# Optimizing a Trainium2 kernel written in Bass

```python
import math
import jax, jax.numpy as jnp
from jax import lax
import numpy as np

D_MODEL = 1024
BATCH = 1
SEQ = 256
DEPTH = 1

N_MEM = 256
ATTN_HEADS = 8
HEAD_DIM = 64
D_ATTN = ATTN_HEADS * HEAD_DIM
D_CONV = D_MODEL - D_ATTN
CONV_WIDTH = 31
Q_BLOCK = 128
MEM_HEADS = 4
MEM_HEAD_DIM = D_MODEL // MEM_HEADS
N_GROUPS = 4
EXPERTS_PER_GROUP = 8
N_EXPERTS = N_GROUPS * EXPERTS_PER_GROUP
TOP_K_IN_GROUP = 2
D_EXPERT = D_MODEL // 2
EPS = 1e-6
OFF_Q = 0
OFF_K = OFF_Q + D_ATTN
OFF_V = OFF_K + D_ATTN
OFF_F = OFF_V + D_ATTN
OFF_C = OFF_F + ATTN_HEADS
D_IN = OFF_C + 2 * D_CONV


def rmsnorm(x, g):
    xf = x.astype(jnp.float32)
    y = xf * lax.rsqrt(jnp.mean(xf * xf, axis=-1, keepdims=True) + EPS)
    return (y * g.astype(jnp.float32)).astype(x.dtype)

def layernorm(x, g, b):
    xf = x.astype(jnp.float32)
    mu = jnp.mean(xf, axis=-1, keepdims=True)
    xc = xf - mu
    y = xc * lax.rsqrt(jnp.mean(xc * xc, axis=-1, keepdims=True) + EPS)
    return (y * g.astype(jnp.float32) + b.astype(jnp.float32)).astype(x.dtype)

def forgetting_attention(q, k, v, log_f):
    S = q.shape[2]
    c = jnp.cumsum(log_f, axis=-1)
    scale = 1.0 / math.sqrt(HEAD_DIM)
    outs = []
    for i in range(S // Q_BLOCK):
        lo, hi = i * Q_BLOCK, (i + 1) * Q_BLOCK
        s = jnp.einsum('bhqd,bhkd->bhqk', q[:, :, lo:hi], k[:, :, :hi]).astype(jnp.float32) * scale
        s = s + c[:, :, lo:hi, None] - c[:, :, None, :hi]
        causal = (lo + jnp.arange(Q_BLOCK))[:, None] >= jnp.arange(hi)[None, :]
        s = jnp.where(causal, s, -jnp.inf)
        p = jax.nn.softmax(s, axis=-1).astype(v.dtype)
        outs.append(jnp.einsum('bhqk,bhkd->bhqd', p, v[:, :, :hi]))
    return jnp.concatenate(outs, axis=2)

def conformer_conv(u, b_glu, w_dw, b_dw, ln_g, ln_b):
    u = u + b_glu
    a, gate = jnp.split(u, 2, axis=-1)
    z = a * jax.nn.sigmoid(gate)
    zp = jnp.pad(z, ((0, 0), (CONV_WIDTH - 1, 0), (0, 0)))
    z = lax.conv_general_dilated(zp, w_dw[:, None, :], window_strides=(1,), padding='VALID',
                                 dimension_numbers=('NWC', 'WIO', 'NWC'),
                                 feature_group_count=D_CONV) + b_dw
    z = layernorm(z, ln_g, ln_b)
    return jax.nn.silu(z)

def parallel_mixer(h, w_in, b_forget, b_glu, w_dw, b_dw, conv_ln_g, conv_ln_b, attn_out_g, w_out):
    B, S, _ = h.shape
    proj = h @ w_in
    def heads(t):
        return t.reshape(B, S, ATTN_HEADS, HEAD_DIM).transpose(0, 2, 1, 3)
    q = heads(proj[..., OFF_Q:OFF_K])
    k = heads(proj[..., OFF_K:OFF_V])
    v = heads(proj[..., OFF_V:OFF_F])
    log_f = jax.nn.log_sigmoid((proj[..., OFF_F:OFF_C] + b_forget).astype(jnp.float32))
    log_f = log_f.transpose(0, 2, 1)
    attn = forgetting_attention(q, k, v, log_f)
    attn = attn.transpose(0, 2, 1, 3).reshape(B, S, D_ATTN)
    attn = rmsnorm(attn, attn_out_g)
    conv = conformer_conv(proj[..., OFF_C:], b_glu, w_dw, b_dw, conv_ln_g, conv_ln_b)
    return jnp.concatenate([attn, conv], axis=-1) @ w_out

def memory_cross_attention(h, mem_n, w_mq, w_mkv, w_mo):
    B, S, _ = h.shape
    q = (h @ w_mq).reshape(B, S, MEM_HEADS, MEM_HEAD_DIM)
    kv = mem_n @ w_mkv
    k, v = jnp.split(kv, 2, axis=-1)
    k = k.reshape(B, -1, MEM_HEADS, MEM_HEAD_DIM)
    v = v.reshape(B, -1, MEM_HEADS, MEM_HEAD_DIM)
    s = jnp.einsum('bshd,bmhd->bhsm', q, k).astype(jnp.float32) / math.sqrt(MEM_HEAD_DIM)
    p = jax.nn.softmax(s, axis=-1).astype(v.dtype)
    o = jnp.einsum('bhsm,bmhd->bshd', p, v).reshape(B, S, D_MODEL)
    return o @ w_mo

def hierarchical_moe(h, w_route_group, b_route_group, w_route_expert, b_route_expert,
                     w_gate, w_up, w_down):
    B, S, D = h.shape
    t = h.reshape(-1, D)
    p_group = jax.nn.softmax((t @ w_route_group).astype(jnp.float32) + b_route_group, axis=-1)
    g_top, g_idx = lax.top_k(p_group, 1)
    e_logits = jnp.einsum('td,gde->tge', t, w_route_expert).astype(jnp.float32) + b_route_expert
    e_logits = jnp.take_along_axis(e_logits, g_idx[:, :, None], axis=1)[:, 0]
    p_exp = jax.nn.softmax(e_logits, axis=-1)
    e_top, e_idx = lax.top_k(p_exp, TOP_K_IN_GROUP)
    w = g_top * e_top / jnp.sum(e_top, axis=-1, keepdims=True)
    ids = g_idx * EXPERTS_PER_GROUP + e_idx
    gates = jnp.sum(jax.nn.one_hot(ids, N_EXPERTS, dtype=jnp.float32) * w[..., None], axis=1)
    gates = gates.astype(h.dtype).T

    def expert_step(y, args):
        wg, wu, wd, ge = args
        out = (jax.nn.silu(t @ wg) * (t @ wu)) @ wd
        return y + ge[:, None] * out, None

    y, _ = lax.scan(expert_step, jnp.zeros_like(t), (w_gate, w_up, w_down, gates))
    return y.reshape(B, S, D)

def first_inputs(seed: int = 0) -> dict:
    key = jax.random.key(seed)
    ks = iter(jax.random.split(key, 32))
    f32 = jnp.float32

    def nrm(shape, fan_in):
        return jax.random.normal(next(ks), shape, f32) * (fan_in ** -0.5)

    def gain(shape):
        return 1.0 + 0.02 * jax.random.normal(next(ks), shape, f32)

    def small(shape):
        return 0.01 * jax.random.normal(next(ks), shape, f32)

    L = DEPTH
    return {
        "x": jax.random.normal(next(ks), (BATCH, SEQ, D_MODEL), f32),
        "mem": jax.random.normal(next(ks), (BATCH, N_MEM, D_MODEL), f32),
        "norm_mix_g": gain((L, D_MODEL)),
        "w_in": nrm((L, D_MODEL, D_IN), D_MODEL),
        "b_forget": jax.random.uniform(next(ks), (L, ATTN_HEADS), f32, 1.0, 6.0),
        "b_glu": small((L, 2 * D_CONV)),
        "w_dw": nrm((L, CONV_WIDTH, D_CONV), CONV_WIDTH),
        "b_dw": small((L, D_CONV)),
        "conv_ln_g": gain((L, D_CONV)),
        "conv_ln_b": small((L, D_CONV)),
        "attn_out_g": gain((L, D_ATTN)),
        "w_out": nrm((L, D_ATTN + D_CONV, D_MODEL), D_ATTN + D_CONV),
        "norm_mem_g": gain((L, D_MODEL)),
        "mem_norm_g": gain((L, D_MODEL)),
        "w_mq": nrm((L, D_MODEL, D_MODEL), D_MODEL),
        "w_mkv": nrm((L, D_MODEL, 2 * D_MODEL), D_MODEL),
        "w_mo": nrm((L, D_MODEL, D_MODEL), D_MODEL),
        "norm_ffn_g": gain((L, D_MODEL)),
        "w_route_group": nrm((L, D_MODEL, N_GROUPS), D_MODEL),
        "b_route_group": small((L, N_GROUPS)),
        "w_route_expert": nrm((L, N_GROUPS, D_MODEL, EXPERTS_PER_GROUP), D_MODEL),
        "b_route_expert": small((L, N_GROUPS, EXPERTS_PER_GROUP)),
        "w_gate": nrm((L, N_EXPERTS, D_MODEL, D_EXPERT), D_MODEL),
        "w_up": nrm((L, N_EXPERTS, D_MODEL, D_EXPERT), D_MODEL),
        "w_down": nrm((L, N_EXPERTS, D_EXPERT, D_MODEL), D_EXPERT),
        "final_g": gain((D_MODEL,)),
    }

def first_block(x, mem, norm_mix_g, w_in, b_forget, b_glu, w_dw, b_dw, conv_ln_g, conv_ln_b,
              attn_out_g, w_out, norm_mem_g, mem_norm_g, w_mq, w_mkv, w_mo, norm_ffn_g,
              w_route_group, b_route_group, w_route_expert, b_route_expert,
              w_gate, w_up, w_down, final_g):
    for l in range(DEPTH):
        h = rmsnorm(x, norm_mix_g[l])
        x = x + parallel_mixer(h, w_in[l], b_forget[l], b_glu[l], w_dw[l], b_dw[l],
                               conv_ln_g[l], conv_ln_b[l], attn_out_g[l], w_out[l])
        h = rmsnorm(x, norm_mem_g[l])
        mem_n = rmsnorm(mem, mem_norm_g[l])
        x = x + memory_cross_attention(h, mem_n, w_mq[l], w_mkv[l], w_mo[l])
        h = rmsnorm(x, norm_ffn_g[l])
        x = x + hierarchical_moe(h, w_route_group[l], b_route_group[l], w_route_expert[l],
                                 b_route_expert[l], w_gate[l], w_up[l], w_down[l])
    return rmsnorm(x, final_g)


DEPTH_2 = 2

N_A = DEPTH_2 // 2
N_B = DEPTH_2 - N_A
D_FF = 2816
LRU_WIDTH = D_MODEL
LRU_BLOCKS = 4
LRU_BW = LRU_WIDTH // LRU_BLOCKS
CONV_W = 4
LRU_C = 8.0
N_HEADS = 16
D_ATTN_2 = N_HEADS * HEAD_DIM


def rms_norm(x, gain):
    xf = x.astype(jnp.float32)
    y = xf * lax.rsqrt(jnp.mean(xf * xf, axis=-1, keepdims=True) + EPS)
    return (y * gain.astype(jnp.float32)).astype(x.dtype)

def swiglu(h, w13, w2):
    gate, up = jnp.split(h @ w13, 2, axis=-1)
    return (jax.nn.silu(gate) * up) @ w2

def causal_depthwise_conv(x, w, b):
    S = x.shape[1]
    xp = jnp.pad(x, ((0, 0), (CONV_W - 1, 0), (0, 0)))
    y = b
    for k in range(CONV_W):
        y = y + w[k] * xp[:, k:k + S]
    return y

def block_diag_linear(x, w, b):
    Bt, S, _ = x.shape
    xb = x.reshape(Bt, S, LRU_BLOCKS, LRU_BW)
    y = jnp.einsum('bsnc,ncd->bsnd', xb, w).reshape(Bt, S, LRU_WIDTH)
    return y + b

def linear_recurrence(a, u):
    def step(h, au):
        a_t, u_t = au
        h = a_t * h + u_t
        return h, h
    h0 = jnp.zeros((a.shape[0], a.shape[2]), jnp.float32)
    _, hs = lax.scan(step, h0, (jnp.swapaxes(a, 0, 1), jnp.swapaxes(u, 0, 1)))
    return jnp.swapaxes(hs, 0, 1)

def rglru_block(h, w_in, conv_w, conv_b, w_r, b_r, w_i, b_i, lam, w_out):
    gate_br, rec = jnp.split(h @ w_in, 2, axis=-1)
    gate_br = jax.nn.gelu(gate_br)
    xc = causal_depthwise_conv(rec, conv_w, conv_b)
    r = jax.nn.sigmoid(block_diag_linear(xc, w_r, b_r))
    i = jax.nn.sigmoid(block_diag_linear(xc, w_i, b_i))
    log_a = -LRU_C * r.astype(jnp.float32) * jax.nn.softplus(-lam.astype(jnp.float32))
    a = jnp.exp(log_a)
    mult = jnp.sqrt(-jnp.expm1(2.0 * log_a))
    u = mult * (i * xc).astype(jnp.float32)
    hs = linear_recurrence(a, u)
    y = hs.astype(h.dtype) * gate_br
    return y @ w_out

def heads(t):
    Bt, S, _ = t.shape
    return t.reshape(Bt, S, N_HEADS, HEAD_DIM).transpose(0, 2, 1, 3)

def shared_kv(x, kv_gain, w_kv, k_gain):
    hkv = rms_norm(x, kv_gain)
    k, v = jnp.split(hkv @ w_kv, 2, axis=-1)
    k = rms_norm(heads(k), k_gain)
    return k, heads(v)

def stick_breaking_attention(q, k, v):
    S = q.shape[2]
    scale = HEAD_DIM ** -0.5
    outs = []
    for blk in range(S // Q_BLOCK):
        q0 = blk * Q_BLOCK
        end = q0 + Q_BLOCK
        z = jnp.einsum('bhqd,bhkd->bhqk', q[:, :, q0:end], k[:, :, :end]).astype(jnp.float32) * scale
        t_pos = q0 + jnp.arange(Q_BLOCK)[:, None]
        s_pos = jnp.arange(end)[None, :]
        mask = s_pos < t_pos
        log_stay = jnp.where(mask, -jax.nn.softplus(z), 0.0)
        stay_after = lax.cumsum(log_stay, axis=3, reverse=True) - log_stay
        log_w = jax.nn.log_sigmoid(z) + stay_after
        w = jnp.where(mask, jnp.exp(log_w), 0.0)
        o = jnp.einsum('bhqk,bhkd->bhqd', w, v[:, :, :end].astype(jnp.float32))
        outs.append(o.astype(v.dtype))
    return jnp.concatenate(outs, axis=2)

def stick_breaking_block(h, k, v, w_q, q_gain, w_o):
    q = rms_norm(heads(h @ w_q), q_gain)
    o = stick_breaking_attention(q, k, v)
    Bt, _, S, _ = o.shape
    o = o.transpose(0, 2, 1, 3).reshape(Bt, S, D_ATTN_2)
    return o @ w_o

def second_inputs(seed: int = 0) -> dict:
    key = jax.random.key(seed)
    keys = jax.random.split(key, 32)
    counter = [0]
    f32 = jnp.float32

    def nk():
        k = keys[counter[0]]
        counter[0] += 1
        return k

    def w(shape, fan_in, scale=1.0):
        return jax.random.normal(nk(), shape, f32) * (scale * fan_in ** -0.5)

    def gain(shape):
        return 1.0 + 0.02 * jax.random.normal(nk(), shape, f32)

    def bias(shape):
        return 0.02 * jax.random.normal(nk(), shape, f32)

    a0 = jax.random.uniform(nk(), (N_A, LRU_WIDTH), f32, 0.9, 0.999)
    return {
        "x": jax.random.normal(nk(), (BATCH, SEQ, D_MODEL), f32),
        "ffn1_norm": gain((DEPTH_2, D_MODEL)),
        "ffn1_w13": w((DEPTH_2, D_MODEL, 2 * D_FF), D_MODEL),
        "ffn1_w2": w((DEPTH_2, D_FF, D_MODEL), D_FF, 0.5),
        "mix_norm": gain((DEPTH_2, D_MODEL)),
        "a_w_in": w((N_A, D_MODEL, 2 * LRU_WIDTH), D_MODEL),
        "a_conv_w": w((N_A, CONV_W, LRU_WIDTH), CONV_W),
        "a_conv_b": bias((N_A, LRU_WIDTH)),
        "a_w_r": w((N_A, LRU_BLOCKS, LRU_BW, LRU_BW), LRU_BW),
        "a_b_r": bias((N_A, LRU_WIDTH)),
        "a_w_i": w((N_A, LRU_BLOCKS, LRU_BW, LRU_BW), LRU_BW),
        "a_b_i": bias((N_A, LRU_WIDTH)),
        "a_lambda": jnp.log(a0) - jnp.log1p(-a0),
        "a_w_out": w((N_A, LRU_WIDTH, D_MODEL), LRU_WIDTH),
        "kv_norm": gain((D_MODEL,)),
        "w_kv": w((D_MODEL, 2 * D_ATTN_2), D_MODEL),
        "k_norm": gain((HEAD_DIM,)),
        "b_w_q": w((N_B, D_MODEL, D_ATTN_2), D_MODEL),
        "q_norm": gain((N_B, HEAD_DIM)),
        "b_w_o": w((N_B, D_ATTN_2, D_MODEL), D_ATTN_2),
        "ffn2_norm": gain((DEPTH_2, D_MODEL)),
        "ffn2_w13": w((DEPTH_2, D_MODEL, 2 * D_FF), D_MODEL),
        "ffn2_w2": w((DEPTH_2, D_FF, D_MODEL), D_FF, 0.5),
    }

def second_block(x, ffn1_norm, ffn1_w13, ffn1_w2, mix_norm, a_w_in, a_conv_w, a_conv_b,
              a_w_r, a_b_r, a_w_i, a_b_i, a_lambda, a_w_out, kv_norm, w_kv, k_norm,
              b_w_q, q_norm, b_w_o, ffn2_norm, ffn2_w13, ffn2_w2):
    k_shared = None
    v_shared = None
    for l in range(DEPTH_2):
        if l == N_A:
            k_shared, v_shared = shared_kv(x, kv_norm, w_kv, k_norm)
        x = x + 0.5 * swiglu(rms_norm(x, ffn1_norm[l]), ffn1_w13[l], ffn1_w2[l])
        h = rms_norm(x, mix_norm[l])
        if l < N_A:
            x = x + rglru_block(h, a_w_in[l], a_conv_w[l], a_conv_b[l], a_w_r[l], a_b_r[l],
                                a_w_i[l], a_b_i[l], a_lambda[l], a_w_out[l])
        else:
            j = l - N_A
            x = x + stick_breaking_block(h, k_shared, v_shared, b_w_q[j], q_norm[j], b_w_o[j])
        x = x + 0.5 * swiglu(rms_norm(x, ffn2_norm[l]), ffn2_w13[l], ffn2_w2[l])
    return x


def setup_inputs(seed=0):
    out = dict(first_inputs(seed))
    for name, value in second_inputs(seed + 1).items():
        if name != "x":
            out[name + "_2"] = value
    return out


def reference(
    x, mem, norm_mix_g, w_in, b_forget, b_glu, w_dw, b_dw, conv_ln_g, conv_ln_b, attn_out_g,
    w_out, norm_mem_g, mem_norm_g, w_mq, w_mkv, w_mo, norm_ffn_g, w_route_group, b_route_group,
    w_route_expert, b_route_expert, w_gate, w_up, w_down, final_g, ffn1_norm_2, ffn1_w13_2,
    ffn1_w2_2, mix_norm_2, a_w_in_2, a_conv_w_2, a_conv_b_2, a_w_r_2, a_b_r_2, a_w_i_2, a_b_i_2,
    a_lambda_2, a_w_out_2, kv_norm_2, w_kv_2, k_norm_2, b_w_q_2, q_norm_2, b_w_o_2, ffn2_norm_2,
    ffn2_w13_2, ffn2_w2_2,
):
    x = first_block(
        x, mem, norm_mix_g, w_in, b_forget, b_glu, w_dw, b_dw, conv_ln_g, conv_ln_b, attn_out_g,
        w_out, norm_mem_g, mem_norm_g, w_mq, w_mkv, w_mo, norm_ffn_g, w_route_group,
        b_route_group, w_route_expert, b_route_expert, w_gate, w_up, w_down, final_g,
    )
    return second_block(
        x, ffn1_norm_2, ffn1_w13_2, ffn1_w2_2, mix_norm_2, a_w_in_2, a_conv_w_2, a_conv_b_2,
        a_w_r_2, a_b_r_2, a_w_i_2, a_b_i_2, a_lambda_2, a_w_out_2, kv_norm_2, w_kv_2, k_norm_2,
        b_w_q_2, q_norm_2, b_w_o_2, ffn2_norm_2, ffn2_w13_2, ffn2_w2_2,
    )


_drawn_inputs = setup_inputs


def setup_inputs(seed=0):
    import zlib

    import numpy as np

    out = dict(_drawn_inputs(seed))
    spreads = {}
    factors = {'b_glu': 2.73,
     'b_dw': 3.006,
     'conv_ln_b': 3.836,
     'norm_mem_g': 4.067,
     'mem_norm_g': 4.84,
     'b_route_group': 13.028,
     'b_route_expert': 8.0,
     'ffn1_norm_2': 8.0,
     'mix_norm_2': 4.137,
     'a_b_r_2': 8.0,
     'a_b_i_2': 8.0,
     'kv_norm_2': 13.921,
     'k_norm_2': 23.426,
     'q_norm_2': 22.182,
     'ffn2_norm_2': 8.0,
     'a_conv_b_2': 2.877}
    for name, (base, spread) in spreads.items():
        noise = np.random.default_rng([zlib.crc32(name.encode()), seed]).standard_normal(out[name].shape)
        drawn = base * np.exp(spread * noise) if base else spread * noise
        out[name] = __import__('jax').numpy.asarray(drawn.astype(out[name].dtype))
    for name, factor in factors.items():
        out[name] = (out[name] * factor).astype(out[name].dtype)
    return out
```

```python
from contextlib import ExitStack

import numpy as np

import concourse.bass as bass
from concourse import mybir

F32 = mybir.dt.float32
I32 = mybir.dt.int32
ACT = mybir.ActivationFunctionType
ALU = mybir.AluOpType
AX = mybir.AxisListType

P = 128
T = 256
TT = T // P
D = 1024
DC = D // P
EPS = 1e-6
BIG = 1e30

HEADS, DH = 8, 64
DA = HEADS * DH
AC = DA // P
TAPS = 31
PAD = 32
MH, MDH = 4, 256
GROUPS, PER = 4, 8
E = GROUPS * PER
PAIRS = E // 2
FE = 512
FEC = FE // P
CAP = 64
NL = GROUPS + E
EP = E + 4
FF = 2816
FC = FF // P
NB = 4
TAPS2 = 4
SH = 16

SLOTS = 6
SLOT = 4096
FPIECE = 3 * D

CONSTS = {}
VECTORS = {}


def columns(table, sizes):
    at = 0
    for name, n in sizes:
        table[name] = (at, n)
        at += n
    return at


NCONST = columns(CONSTS, [
    ("ident", P), ("ones", P), ("before", P), ("after", P), ("headsum", P), ("causal", 3 * P),
    ("stick", 3 * P), ("slots", CAP), ("first8", PER), ("first4", GROUPS), ("passes", 4),
    ("neghalf", TT), ("eps", 1), ("scan1", T), ("keyside", 4 * T), ("queryside", T), ("pick", 8)])
NVEC = columns(VECTORS, [
    ("norm_mix", 8), ("b_glu", 8), ("w_dw", TAPS * 4), ("b_dw", 4), ("ln_g", 4), ("ln_b", 4),
    ("attn_g", 4), ("norm_mem", 8), ("mem_norm", 8), ("norm_ffn", 8), ("final", 8), ("b_forget", 1),
    ("ffn1_0", 8), ("ffn1_1", 8), ("mix_0", 8), ("mix_1", 8), ("conv_w", TAPS2 * 8), ("conv_b", 8),
    ("b_r", 8), ("b_i", 8), ("lam", 8), ("kv", 8), ("k_gain", 1), ("q_gain", 1), ("ffn2_0", 8),
    ("ffn2_1", 8), ("b_route", NL)])


def constants():
    c = np.zeros((P, NCONST), np.float32)

    def put(name, value):
        at, n = CONSTS[name]
        c[:, at:at + n] = value

    row, col = np.arange(P)[:, None], np.arange(P)[None, :]
    put("ident", row == col)
    put("ones", 1)
    put("before", row < col)
    put("after", row > col)
    put("headsum", row // DH == col // DH)
    tri = np.where(col <= row, 0, -BIG)
    put("causal", np.concatenate([tri, np.zeros((P, P)), tri], 1))
    put("stick", np.concatenate([row < np.arange(T)[None, :], row < col], 1))
    put("slots", np.arange(CAP))
    put("first8", PER - np.arange(PER))
    put("first4", GROUPS - np.arange(GROUPS))
    put("passes", CAP * np.arange(4))
    put("neghalf", -0.5)
    put("eps", EPS)
    put("scan1", 1)
    key = np.zeros((P, 4, T), np.float32)
    pick = np.zeros((P, 2, 4), np.float32)
    for j in range(4):
        key[2 * j, j] = 1
        key[DH + 2 * j + 1, j] = 1
        pick[2 * j, 0, j] = -1
        pick[2 * j + 1, 1, j] = -1
    put("keyside", key.reshape(P, -1))
    put("pick", pick.reshape(P, -1))
    query = np.zeros((P, T), np.float32)
    query[32:40] = 1
    query[DH + 32:DH + 40] = 1
    put("queryside", query)
    return c



class Tile:

    def __init__(self, n, bank, engine, emptied, before):
        self.n, self.bank, self.engine, self.emptied, self.before = n, bank, engine, emptied, before


class Plan:
    def __init__(self):
        self.tiles, self.stage = [], {}
        self.last = {}
        self.count = {"act": 0, "dve": 0}
        self.pieces = []
        self.first = {}
        self.filled = [0] * SLOTS

    def add(self, stage, engines, banks=None):
        out = []
        for i, engine in enumerate(engines):
            n = len(self.tiles)
            bank = banks[i] if banks else n % 4
            self.count[engine] += 1
            t = Tile(n, bank, engine, self.count[engine], self.last.get(bank))
            self.last[bank] = t
            self.tiles.append(t)
            out.append(t)
        self.stage[stage] = out

    def piece(self, stage, source, index, floats, freed):
        n = len(self.pieces)
        self.first.setdefault(stage, n)
        self.filled[n % SLOTS] += 16
        self.pieces.append((source, index, floats, freed, self.filled[n % SLOTS]))

    def stream(self, stage, source, at, tiles_a_piece):
        tiles = self.stage[stage]
        for j in range(0, len(tiles), tiles_a_piece):
            last = tiles[min(j + tiles_a_piece, len(tiles)) - 1]
            self.piece(stage, source, at + j // tiles_a_piece, SLOT, ("tile_done", last.n + 1))
        return at + -(-len(tiles) // tiles_a_piece)


def make_plan():
    p = Plan()
    p.add("forget", ["dve"])
    p.add("glu", ["act", "dve"] * 4)
    p.add("memk", ["act"] * 8)
    p.add("memv", ["act"] * 4)
    p.add("q", ["act"] * 4)
    p.add("k", ["act"] * 4)
    p.add("v", ["act"] * 2)
    p.add("wout", ["dve"] * 8)
    p.add("mq", ["act"] * 8)
    p.add("mo", ["dve"] * 8)
    p.add("htok", ["act"] * 4)
    p.add("route", ["dve"])
    p.add("rank", ["dve"])
    p.add("maxrank", ["dve"])
    p.add("ffn0", ["dve"] * 4, range(4))
    p.add("rec", ["act"] * 8)
    p.add("gate", ["act"] * 8)
    p.add("r", ["act"] * 8)
    p.add("i", ["act"] * 8)
    p.add("aout", ["dve"] * 8)
    p.add("ffn1", ["dve"] * 4, range(4))
    p.add("kvk", ["act"] * 8)
    p.add("kvv", ["act"] * 4)
    p.add("ffn2", ["dve"] * 4, range(4))
    p.add("bq", ["act"] * 8)
    p.add("bo", ["dve"] * 8)
    p.add("ffn3", ["dve"] * 4, range(4))

    for j in range(2):
        p.piece("glu", "stream", j, SLOT, ("tile_done", p.stage["glu"][6 + j].n + 1))
    at = 2
    at = p.stream("memk", "stream", at, 4)
    at = p.stream("memv", "stream", at, 2)
    at = p.stream("q", "stream", at, 4)
    at = p.stream("k", "stream", at, 4)
    at = p.stream("v", "stream", at, 2)
    at = p.stream("wout", "stream", at, 4)
    at = p.stream("mq", "stream", at, 4)
    at = p.stream("mo", "stream", at, 4)
    for n in range(PAIRS):
        for source, e in [("gate", 0), ("gate", 1), ("up", 0), ("up", 1), ("down", 0), ("down", 1)]:
            freed = {"gate": ("hidden_done", 2 * n + 1), "up": ("hidden_done", 2 * n + 2), "down": ("y_done", 2 * n + 2)}[source]
            p.piece("moe", source, 2 * n + e, SLOT, freed)

    def ffn(which):
        for j in range(FC):
            freed = ("down_done", (FC - 1) * which + j + 2) if j < FC - 1 else \
                ("tile_done", p.stage[f"ffn{which}"][3].n + 1)
            p.piece(f"ffn{which}", "ffn", FC * which + j, FPIECE, freed)

    ffn(0)
    at = p.stream("rec", "stream", at, 4)
    at = p.stream("gate", "stream", at, 4)
    p.piece("r", "stream", at, SLOT, ("tile_done", p.stage["i"][7].n + 1))
    at += 1
    at = p.stream("aout", "stream", at, 4)
    ffn(1)
    at = p.stream("kvk", "stream", at, 4)
    at = p.stream("kvv", "stream", at, 2)
    ffn(2)
    at = p.stream("bq", "stream", at, 4)
    at = p.stream("bo", "stream", at, 4)
    ffn(3)
    p.streamed = at
    return p


NORMS = [("mem", 8), ("mix", 8), ("attn", 4), ("conv", 4), ("memq", 8), ("moe", 8), ("final", 8),
         ("ffn0", 8), ("lru", 8), ("ffn1", 8), ("kv", 8), ("ffn2", 8), ("stick", 8), ("ffn3", 8)]
NORM = {}
_at = 0
for _n, (_name, _chunks) in enumerate(NORMS):
    NORM[_name] = (_n, _chunks, _at)
    _at += _chunks


def two_blocks(nc, xT, memT, consts, vectors, w_forget, w_route, stream, ffn, w_gate, w_up, w_down, out):
    plan = make_plan()
    sources = {"stream": stream, "ffn": ffn, "gate": w_gate, "up": w_up, "down": w_down}

    with ExitStack() as ctx:
        def sb(name, shape, dt=F32):
            return ctx.enter_context(nc.sbuf_tensor(name, shape, dt))

        def sem(name):
            return ctx.enter_context(nc.semaphore(name))

        ring = sb("ring", [P, SLOTS, SLOT])
        X = sb("X", [P, DC, T])
        H = sb("H", [P, DC, T])
        SQ = sb("SQ", [P, DC, T])
        B1 = sb("B1", [P, DC, T])
        B2 = sb("B2", [P, DC, T])
        B3 = sb("B3", [P, DC, T])
        B4 = sb("B4", [P, DC, T])
        B5 = sb("B5", [P, DC, T])
        B6 = sb("B6", [P, DC, T])
        zin = sb("zin", [P, DC, T + PAD])
        C = sb("C", [P, NCONST])
        V = sb("V", [P, NVEC])
        wf = sb("wf", [P, DC, HEADS])
        wr = sb("wr", [P, DC, NL])
        ms = sb("ms", [P, TT])
        rs = sb("rs", [P, TT])
        diag = sb("diag", [P, T])
        small = B5[:, 4:8, :]
        work = sb("work", [P, 6, 512])
        negmax = sb("negmax", [P, 2, TT])
        rowsum = sb("rowsum", [P, 2, TT])
        rowinv = sb("rowinv", [P, 2, TT])
        hid = B5[:, 0:3, :]
        act2 = B6[:, 0:2, :]
        spl = sb("spl", [P, 4, DC])
        qg = sb("qg", [P, 1])
        lg = sb("lg", [P, TT, NL])
        r4 = sb("r4", [P, 6, TT, GROUPS])
        r8 = sb("r8", [P, 8, TT, PER])
        r1 = sb("r1", [P, 12, TT])
        pick32 = sb("pick32", [P, TT, PER, GROUPS])
        chosen = sb("chosen", [P, TT, E])
        rank = sb("rank", [P, TT, EP])
        gates = sb("gates", [P, TT, EP])
        mr = sb("mr", [P, 2])
        mrow = sb("mrow", [1, 8])
        npass = sb("npass", [1, 1], I32)
        disp = B3[:, 4, :].rearrange("p (t e s) -> p t e s", t=TT, e=2)
        comb = B3[:, 5, :].rearrange("p (t e s) -> p t e s", t=TT, e=2)
        back = B3[:, 6, :]
        esilu = B2[:, 4:6, :].rearrange("p c t -> p (c t)")
        eprod = B2[:, 6:8, :].rearrange("p c t -> p (c t)")
        ehid = B4[:, 0:2, :].rearrange("p c (a s) -> p (c a) s", a=2)
        XG = B2[:, 0:4, :].rearrange("p c (a s) -> p (c a) s", a=2)
        Y = B3[:, 0:4, :].rearrange("p a t -> p (a t)")
        htok = B1[:, :, :].rearrange("p a t -> p (a t)").rearrange("p (t d) -> p t d", t=TT)

        ps = ctx.enter_context(nc.psum_tensor("ps", [P, 8, 512], F32))

        def bank(b):
            return ps[:, b, :]

        def const(name):
            at, n = CONSTS[name]
            return C[:, at:at + n]

        def vec(name, i=0):
            at, _ = VECTORS[name]
            return V[:, at + i:at + i + 1]

        ident, ones = const("ident"), const("ones")

        loaded = [sem(f"slot{i}_loaded") for i in range(SLOTS)]
        inputs_loaded = [sem(f"input{i}_loaded") for i in range(6)]
        tile_done = sem("tile_done")
        taken = {"act": sem("taken_by_act"), "dve": sem("taken_by_dve")}
        prepared = sem("prepared")
        square_done = sem("square_done")
        msum_done = sem("msum_done")
        ms_ready = sem("ms_ready")
        rs_ready = sem("rs_ready")
        diag_ready = sem("diag_ready")
        rbcast_done = sem("rbcast_done")
        normed = sem("normed")
        vstep = sem("vector_step")
        astep = sem("scalar_step")
        forget_exp = sem("forget_exp")
        bias_ready = sem("bias_ready")
        glu_gate = sem("glu_gate")
        conv_step = sem("conv_step")
        mean_done = sem("mean_done")
        centred = sem("centred")
        conv_out = sem("conv_out")
        score_done = sem("score_done")
        score_read = sem("score_read")
        max_ready = sem("max_ready")
        exp_done = sem("exp_done")
        prob_ready = sem("prob_ready")
        turned = sem("turned")
        turned_copied = sem("turned_copied")
        o_done = sem("o_done")
        o_copied = sem("o_copied")
        down_done = sem("down_done")
        gu_done = sem("gu_done")
        ffn_silu = sem("ffn_silu")
        hid_ready = sem("hid_ready")
        lam_ready = sem("lam_ready")
        xconv_ready = sem("xconv_ready")
        decay_ready = sem("decay_ready")
        ssq_ready = sem("ssq_ready")
        root_ready = sem("root_ready")
        lru_out = sem("lru_out")
        headsq = sem("headsq")
        headsum_done = sem("headsum_done")
        headroot = sem("headroot")
        head_ready = sem("head_ready")
        z_done = sem("z_done")
        log1p_ready = sem("log1p_ready")
        stay_in = sem("stay_in")
        stay_done = sem("stay_done")
        logw_ready = sem("logw_ready")
        w_exp = sem("w_exp")
        w_ready = sem("w_ready")
        so_done = sem("so_done")
        so_copied = sem("so_copied")
        router_exp = sem("router_exp")
        router_in = sem("router_in")
        chosen_ready = sem("chosen_ready")
        maxrank_in = sem("maxrank_in")
        npass_ready = sem("npass_ready")
        stored = sem("stored")

        class Moe:

            def __init__(self, tag):
                self.disp_ready = sem(f"{tag}disp_ready")
                self.gathered = sem(f"{tag}gathered")
                self.xg_ready = sem(f"{tag}xg_ready")
                self.comb_turned = sem(f"{tag}comb_turned")
                self.back_ready = sem(f"{tag}back_ready")
                self.hidden_done = sem(f"{tag}hidden_done")
                self.esilu_ready = sem(f"{tag}esilu_ready")
                self.eprod_ready = sem(f"{tag}eprod_ready")
                self.hidden_turned = sem(f"{tag}hidden_turned")
                self.ehid_ready = sem(f"{tag}ehid_ready")
                self.y_done = sem(f"{tag}y_done")
                self.y_ready = sem(f"{tag}y_ready")
                self.spread_done = sem(f"{tag}spread_done")
                self.spread_taken = sem(f"{tag}spread_taken")

        hot, cold = Moe("main_"), Moe("more_")
        cold_loaded = sem("more_loaded")
        shifted = sem("ranks_shifted")
        by_name = {"tile_done": tile_done, "hidden_done": hot.hidden_done, "y_done": hot.y_done,
                   "down_done": down_done}

        block = ctx.enter_context(nc.Block())

        def slot_of(stage, j):
            n = plan.first[stage] + j
            return n % SLOTS

        def wait_piece(eng, stage, j):
            n = plan.first[stage] + j
            eng.wait_ge(loaded[n % SLOTS], plan.pieces[n][4])

        def piece(stage, j, k):
            return ring[:, slot_of(stage, j), :].rearrange("p (k n) -> p k n", k=k)

        def wait_taken(eng, tile):
            eng.wait_ge(taken[tile.engine], tile.emptied)

        def moe_slots(n0=0):
            return [(plan.first["moe"] + j) % SLOTS for j in range(SLOTS)]

        S_G0, S_G1, S_U0, S_U1, S_D0, S_D1 = moe_slots()
        MOE_BASE = {(plan.first["moe"] + j) % SLOTS: plan.pieces[plan.first["moe"] + j][4] - 16 for j in range(SLOTS)}

        @block.sync
        def _(sp):
            def load(n):
                source, index, floats, _, _ = plan.pieces[n]
                if n >= SLOTS:
                    name, value = plan.pieces[n - SLOTS][3]
                    sp.wait_ge(by_name[name], value)
                sp.dma_start(ring[:, n % SLOTS, 0:floats], sources[source][index]).then_inc(loaded[n % SLOTS], 16)

            for n in range(plan.first["moe"] + SLOTS):
                load(n)

            MOE_ORDER = [(w_gate, 0), (w_gate, 1), (w_up, 0), (w_up, 1), (w_down, 0), (w_down, 1)]
            with sp.Fori(1, PAIRS) as n:
                for j, (source, e) in enumerate(MOE_ORDER):
                    s = (plan.first["moe"] + j) % SLOTS
                    if j < 4:
                        sp.wait_ge(hot.hidden_done, 2 * n - 1 + j // 2)
                    else:
                        sp.wait_ge(hot.y_done, 2 * n)
                    sp.dma_start(ring[:, s, :], source[2 * n + e]).then_inc(loaded[s], 16)
            sp.wait_ge(npass_ready, 1)
            passes = sp.value_load(npass[0:1, 0:1], min_val=1, max_val=4)
            with sp.If(passes > 1):
                sp.wait_ge(hot.y_done, E)
                with sp.Fori(1, passes) as q:
                    with sp.Fori(0, PAIRS) as n:
                        sp.wait_ge(cold.y_done, (q - 1) * E + 2 * n + 1)
                        for j, (source, e) in enumerate(MOE_ORDER):
                            s = (plan.first["moe"] + j) % SLOTS
                            sp.dma_start(ring[:, s, :], source[2 * n + e]).then_inc(cold_loaded, 16)
                sp.wait_ge(chosen_ready, 2)
            start = plan.first["ffn0"]

            def ffn_loads(which):
                base = plan.first[f"ffn{which}"]
                head = SLOTS + (FC - SLOTS) % SLOTS
                for j in range(head):
                    load(base + j)
                with sp.Fori(0, (FC - head) // SLOTS) as i:
                    for j in range(SLOTS):
                        n = base + head + j
                        sp.wait_ge(down_done, 6 * i + (FC - 1) * which + head + j - SLOTS + 2)
                        sp.dma_start(ring[:, n % SLOTS, 0:FPIECE], ffn[6 * i + FC * which + head + j]).then_inc(loaded[n % SLOTS], 16)

            n = start
            for which in range(4):
                while n < plan.first[f"ffn{which}"]:
                    load(n)
                    n += 1
                ffn_loads(which)
                n += FC
            last = plan.stage["ffn3"]
            for b in range(4):
                wait_taken(sp, last[b])
                sp.dma_start(out[:, 2 * b * T:(2 * b + 2) * T], X[:, 2 * b:2 * b + 2, :].rearrange("p c t -> p (c t)")).then_inc(stored, 16)
            sp.wait_ge(stored, 4 * 16)

        @block.gpsimd
        def _(pool):
            pool.memset(zin[:, :, 0:PAD], 0.0).then_inc(prepared, 1)
            pool.memset(rank[:, :, :], -1.0).then_inc(prepared, 1)
            pool.memset(gates[:, :, :], 0.0).then_inc(prepared, 1)
            pool.wait_ge(inputs_loaded[0], 16)
            for n in range(len(NORMS)):
                pool.wait_ge(ms_ready, n + 1)
                if n:
                    pool.wait_ge(diag_ready, TT * n)
                pool.tensor_tensor(rs[:, :], ms[:, :], const("neghalf"), ALU.pow).then_inc(rs_ready, 1)

        @block.scalar
        def _(act):
            steps = [0]
            act.nop().then_inc(hot.y_ready, 1)
            act.nop().then_inc(hot.back_ready, 1)

            def step(ins):
                ins.then_inc(astep, 1)
                steps[0] += 1
                act.wait_ge(astep, steps[0])

            for i, (dst, src) in enumerate([(C[:, :], consts), (V[:, :], vectors), (X[:, :, :].rearrange("p c t -> p (c t)"), xT),
                                            (B3[:, :, :].rearrange("p c t -> p (c t)"), memT),
                                            (wf[:, :, :].rearrange("p c h -> p (c h)"), w_forget),
                                            (wr[:, :, :].rearrange("p c h -> p (c h)"), w_route)]):
                act.dma_start(dst, src).then_inc(inputs_loaded[i], 16)

            def squares(name, src, ready):
                n, chunks, base = NORM[name]
                if n:
                    act.wait_ge(msum_done, n)
                for c in range(chunks):
                    ready(c)
                    act.activation(SQ[:, c, :], src(c), ACT.Square).then_inc(square_done, 1)

            def take(stage, i, dst, func=ACT.Copy, scale=1.0, bias=None, cols=T, rows=P):
                t = plan.stage[stage][i]
                act.wait_ge(tile_done, t.n + 1)
                extra = {} if bias is None else {"bias": bias}
                act.activation(dst, bank(t.bank)[0:rows, 0:cols], func, scale=scale, **extra).then_inc(taken["act"], 1)

            squares("mem", lambda c: B3[:, c, :], lambda c: act.wait_ge(inputs_loaded[3], 16))
            squares("mix", lambda c: X[:, c, :], lambda c: act.wait_ge(inputs_loaded[2], 16))
            act.wait_ge(inputs_loaded[1], 16)
            act.wait_ge(taken["dve"], plan.stage["forget"][0].emptied)
            step(act.activation(small[0:HEADS, 1, :], small[0:HEADS, 0, :], ACT.Abs))
            step(act.activation(small[0:HEADS, 1, :], small[0:HEADS, 1, :], ACT.Exp, scale=-1.0))
            act.activation(small[0:HEADS, 2, :], small[0:HEADS, 1, :], ACT.Ln, bias=1.0).then_inc(forget_exp, 1)
            at = VECTORS["lam"][0]
            step(act.activation(spl[:, 0, :], V[:, at:at + DC], ACT.Abs))
            step(act.activation(spl[:, 0, :], spl[:, 0, :], ACT.Exp, scale=-1.0))
            act.activation(spl[:, 1, :], spl[:, 0, :], ACT.Ln, bias=1.0).then_inc(lam_ready, 1)
            for c in range(AC):
                t = plan.stage["glu"][2 * c]
                act.wait_ge(tile_done, t.n + 1)
                act.activation(B6[:, 4 + c, :], bank(t.bank)[:, 0:T], ACT.Sigmoid, bias=vec("b_glu", 4 + c)).then_inc(taken["act"], 1)
            for m in range(8):
                take("memk", m, B1[:, m, :])
            memv = B2[:, :, :].rearrange("p c t -> p (c t)").rearrange("p (t d) -> p t d", t=TT)
            for m in range(4):
                take("memv", m, memv[:, m % 2, (m // 2) * 512:(m // 2 + 1) * 512], cols=512)
            for m in range(4):
                take("q", m, B4[:, m, :], scale=DH ** -0.5)
            for m in range(4):
                take("k", m, B4[:, 4 + m, :])
            v1 = B5[:, 0:4, :].rearrange("p c t -> p (c t)").rearrange("p (t d) -> p t d", t=TT)
            for m in range(2):
                take("v", m, v1[:, m, :], cols=512)

            def softmax_exp(g, src, widths):
                act.wait_ge(max_ready, g + 1)
                if g >= 2:
                    act.wait_ge(turned, g - 1)
                at = 0
                for t, w in enumerate(widths):
                    act.activation(work[:, g % 2, at:at + w], src[:, at:at + w], ACT.Exp, bias=negmax[:, g % 2, t:t + 1],
                                   accum_out=rowsum[:, g % 2, t:t + 1]).then_inc(exp_done, 1)
                    at += w

            def turned_copy(g, cols):
                act.wait_ge(turned, g + 1)
                act.activation(work[:, 2 + g % 2, 0:cols], bank(6)[:, 0:cols], ACT.Copy).then_inc(turned_copied, 1)

            for s in range(HEADS + 2):
                if s < HEADS:
                    softmax_exp(s, work[:, s % 2, :], [P, T])
                if 1 <= s <= HEADS:
                    turned_copy(s - 1, 3 * P)
                if s >= 2 and s % 2 == 1:
                    j = (s - 2) // 2
                    act.wait_ge(o_done, j + 1)
                    act.activation(B3[:, j, :], bank(7)[:, 0:T], ACT.Copy).then_inc(o_copied, 1)
            squares("attn", lambda c: B3[:, c, :], lambda c: act.wait_ge(o_copied, c + 1))
            squares("conv", lambda c: B5[:, 4 + c, :], lambda c: act.wait_ge(centred, c + 1))
            for c in range(AC):
                act.wait_ge(normed, NORM["conv"][2] + c + 1)
                act.activation(B6[:, 4 + c, :], B6[:, 4 + c, :], ACT.Silu, bias=vec("ln_b", c)).then_inc(conv_out, 1)

            def residual(stage):
                return lambda c: wait_taken(act, plan.stage[stage][c])

            squares("memq", lambda c: X[:, c, :], residual("wout"))
            for m in range(8):
                take("mq", m, B4[:, m, :], scale=MDH ** -0.5)
            for s in range(MH + 2):
                g = HEADS + s
                if s < MH:
                    softmax_exp(g, bank(4 + g % 2), [T, T])
                if 1 <= s <= MH:
                    turned_copy(g - 1, 512)
                if s >= 2:
                    act.wait_ge(o_done, HEADS // 2 + s - 1)
                    act.activation(B5[:, 2 * (s - 2):2 * (s - 2) + 2, :].rearrange("p c t -> p (c t)"), bank(7)[:, :], ACT.Copy).then_inc(o_copied, 1)
            squares("moe", lambda c: X[:, c, :], residual("mo"))
            for m in range(4):
                take("htok", m, htok[:, m // 2, (m % 2) * 512:(m % 2 + 1) * 512], cols=512)
            act.wait_ge(router_in, 1)
            act.activation(r4[:, 1, :, :], r4[:, 0, :, :], ACT.Exp).then_inc(router_exp, 1)
            act.wait_ge(router_in, 2)
            act.activation(r1[:, 6, :], r1[:, 5, :], ACT.Exp).then_inc(router_exp, 1)

            def xg_copy(S, k):
                for b in range(2):
                    act.wait_ge(S.gathered, 2 * k + b + 1)
                    act.activation(XG[:, 4 * b:4 * b + 4, :].rearrange("p c t -> p (c t)"), bank(1 + 2 * b), ACT.Copy).then_inc(S.xg_ready, 1)

            def silu(S, k):
                act.wait_ge(S.hidden_done, 2 * k + 1)
                act.activation(esilu, bank(3), ACT.Silu).then_inc(S.esilu_ready, 1)

            def hidden_copy(S, k):
                act.wait_ge(S.hidden_turned, k + 1)
                act.activation(ehid.rearrange("p f s -> p (f s)"), bank(0), ACT.Copy).then_inc(S.ehid_ready, 1)

            def back_copy(S, k):
                act.wait_ge(S.comb_turned, k + 1)
                act.activation(back[:, :], bank(2)[:, 0:T], ACT.Copy).then_inc(S.back_ready, 1)

            def y_copy(S, k, more):
                for b in range(2):
                    act.wait_ge(S.y_done, 2 * k + b + 1 + more)
                    act.activation(Y[:, b * 512:(b + 1) * 512], bank(5 + b), ACT.Copy).then_inc(S.y_ready, 1)

            xg_copy(hot, 0)
            with act.Fori(0, PAIRS) as n:
                silu(hot, n)
                hidden_copy(hot, n)
                xg_copy(hot, n + 1)
                back_copy(hot, n)
                y_copy(hot, n, 0)
            act.wait_ge(npass_ready, 1)
            passes = act.value_load(npass[0:1, 0:1], min_val=1, max_val=4)
            with act.If(passes > 1):
                with act.Fori(1, passes) as q:
                    with act.Fori(0, PAIRS) as n:
                        k = (q - 1) * PAIRS + n
                        xg_copy(cold, k)
                        back_copy(cold, k)
                        silu(cold, k)
                        hidden_copy(cold, k)
                        y_copy(cold, k, 1)
            def after_moe(c):
                act.wait_ge(chosen_ready, 2)

            squares("final", lambda c: X[:, c, :], after_moe)

            def swiglu(which):
                def one(j, base, i=0):
                    act.wait_ge(gu_done, base + j + 1 + i)
                    act.activation(act2[:, j % 2, :], bank(4 + j % 2)[:, 0:T], ACT.Silu).then_inc(ffn_silu, 1)
                base = FC * which
                for j in range(2):
                    one(j, base)
                with act.Fori(0, 3) as i:
                    for j in range(2, 8):
                        one(j, base, 6 * i)
                for j in range(20, FC):
                    one(j, base)

            squares("ffn0", lambda c: X[:, c, :], lambda c: act.wait_ge(normed, NORM["final"][2] + c + 1))
            swiglu(0)

            def residual_ffn(which):
                return lambda c: wait_taken(act, plan.stage[f"ffn{which}"][c // 2])

            squares("lru", lambda c: X[:, c, :], residual_ffn(0))
            for m in range(8):
                take("rec", m, zin[:, m, PAD:PAD + T])
            for m in range(8):
                take("gate", m, B2[:, m, :], func=ACT.Gelu_apprx_tanh)
            for m in range(8):
                take("r", m, B3[:, m, :], func=ACT.Sigmoid, bias=vec("b_r", m))
            for m in range(8):
                take("i", m, B4[:, m, :], func=ACT.Sigmoid, bias=vec("b_i", m))
            act.wait_ge(lam_ready, 2)
            for m in range(8):
                act.wait_ge(taken["act"], plan.stage["r"][m].emptied)
                act.activation(B5[:, m, :], B3[:, m, :], ACT.Exp, scale=spl[:, 3, m:m + 1]).then_inc(decay_ready, 1)
                act.activation(B6[:, m, :], B3[:, m, :], ACT.Tanh, scale=spl[:, 3, m:m + 1]).then_inc(decay_ready, 1)
            for m in range(8):
                act.wait_ge(ssq_ready, m + 1)
                act.activation(B6[:, m, :], B6[:, m, :], ACT.Sqrt, scale=-1.0).then_inc(root_ready, 1)
            squares("ffn1", lambda c: X[:, c, :], residual("aout"))
            swiglu(1)
            squares("kv", lambda c: X[:, c, :], residual_ffn(1))

            def head_norm(stage, dst, base):
                def root(m):
                    act.wait_ge(headsum_done, base + m + 1)
                    if base + m >= 2:
                        act.wait_ge(head_ready, base + m - 1)
                    act.activation(work[:, 2 + m % 2, 0:T], bank(4 + m % 2)[:, 0:T], ACT.Sqrt, scale=1.0 / DH,
                                   bias=const("eps")).then_inc(headroot, 1)

                for m in range(8):
                    t = plan.stage[stage][m]
                    act.wait_ge(tile_done, t.n + 1)
                    act.activation(dst[:, m, :], bank(t.bank)[:, 0:T], ACT.Copy).then_inc(headsq, 1)
                    if m >= 2:
                        act.wait_ge(headsum_done, base + m - 1)
                    act.activation(work[:, m % 2, 0:T], bank(t.bank)[:, 0:T], ACT.Square).then_inc(taken["act"], 1)
                    if m >= 1:
                        root(m - 1)
                root(7)

            head_norm("kvk", B1, 0)
            for m in range(4):
                take("kvv", m, memv[:, m % 2, (m // 2) * 512:(m // 2 + 1) * 512], cols=512)
            squares("ffn2", lambda c: X[:, c, :], residual_ffn(1))
            swiglu(2)
            squares("stick", lambda c: X[:, c, :], residual_ffn(2))
            head_norm("bq", B3, 8)

            for s in range(SH + 2):
                if s < SH:
                    act.wait_ge(z_done, s + 1)
                    if s >= 2:
                        act.wait_ge(logw_ready, s - 1)
                    z, l = work[:, s % 2, 0:3 * P], work[:, 2 + s % 2, 0:3 * P]
                    act.activation(z, bank(4 + s % 2)[:, 0:3 * P], ACT.Copy).then_inc(log1p_ready, 1)
                    step(act.activation(l, bank(4 + s % 2)[:, 0:3 * P], ACT.Abs))
                    step(act.activation(l, l, ACT.Exp, scale=-1.0))
                    act.activation(l, l, ACT.Ln, bias=1.0).then_inc(log1p_ready, 1)
                if 1 <= s <= SH:
                    h = s - 1
                    act.wait_ge(logw_ready, h + 1)
                    act.activation(B5[:, 4 + 2 * (h % 2):6 + 2 * (h % 2), :].rearrange("p c t -> p (c t)")[:, 0:3 * P],
                                   B5[:, 4 + 2 * (h % 2):6 + 2 * (h % 2), :].rearrange("p c t -> p (c t)")[:, 0:3 * P], ACT.Exp).then_inc(w_exp, 1)
                if s >= 2 and s % 2 == 1:
                    j = (s - 2) // 2
                    act.wait_ge(so_done, 2 * (j + 1))
                    act.activation(B4[:, j, :], bank(7)[:, 0:T], ACT.Copy).then_inc(so_copied, 1)
            squares("ffn3", lambda c: X[:, c, :], residual("bo"))
            swiglu(3)

        @block.tensor
        def _(pe):
            def norm(name):
                n, chunks, base = NORM[name]
                if n:
                    pe.wait_ge(ms_ready, n)
                for c in range(chunks):
                    pe.wait_ge(square_done, base + c + 1)
                    for t in range(TT):
                        last = pe.matmul(bank(6)[:, t:t + 1], SQ[:, c, t * P:(t + 1) * P], ones[:, 0:1],
                                         start=(c == 0 and t == 0), stop=(c == chunks - 1), skip_group_check=True)
                last.then_inc(msum_done, 1)
                pe.wait_ge(diag_ready, TT * (n + 1))
                if n:
                    pe.wait_ge(normed, base)
                pe.matmul(bank(7)[:, 0:T], ones, diag[:, :], start=True, stop=True).then_inc(rbcast_done, 1)

            def open_tile(t):
                if t.before:
                    wait_taken(pe, t.before)

            def project(stage, src, ready, chunks=DC, per=4, first=0):
                for m, t in enumerate(plan.stage[stage]):
                    if m % per == 0:
                        wait_piece(pe, stage, first + m // per)
                    open_tile(t)
                    w = piece(stage, first + m // per, DC)
                    for c in range(chunks):
                        if m == 0:
                            ready(c)
                        last = pe.matmul(bank(t.bank)[:, 0:T], w[:, c, (m % per) * P:(m % per + 1) * P], src(c),
                                         start=(c == 0), stop=(c == chunks - 1))
                    last.then_inc(tile_done, 1)

            def values(stage, src, halves):
                order = [(t, h) for h in range(halves) for t in range(TT)]
                for h in range(halves):
                    wait_piece(pe, stage, h)
                for (tt, h), t in zip(order, plan.stage[stage]):
                    open_tile(t)
                    w = piece(stage, h, DC)
                    for c in range(DC):
                        last = pe.matmul(bank(t.bank), src[:, c, tt * P:(tt + 1) * P], w[:, c, :],
                                         start=(c == 0), stop=(c == DC - 1))
                    last.then_inc(tile_done, 1)

            def is_normed(name):
                base = NORM[name][2]
                return lambda c: pe.wait_ge(normed, base + c + 1)

            def chunk(buf):
                return lambda c: buf[:, c, :]

            pe.nop().then_inc(down_done, 1)
            pe.nop().then_inc(cold.y_done, 1)

            pe.wait_ge(inputs_loaded[0], 16)
            norm("mem")
            norm("mix")
            t = plan.stage["forget"][0]
            pe.wait_ge(inputs_loaded[4], 16)
            for c in range(DC):
                pe.wait_ge(normed, NORM["mix"][2] + c + 1)
                last = pe.matmul(bank(t.bank)[0:HEADS, 0:T], wf[:, c, :], H[:, c, :], start=(c == 0), stop=(c == DC - 1))
            last.then_inc(tile_done, 1)
            wait_piece(pe, "glu", 0)
            wait_piece(pe, "glu", 1)
            for m, t in enumerate(plan.stage["glu"]):
                open_tile(t)
                w = piece("glu", m % 2, DC)
                for c in range(DC):
                    last = pe.matmul(bank(t.bank)[:, 0:T], w[:, c, (m // 2) * P:(m // 2 + 1) * P], H[:, c, :],
                                     start=(c == 0), stop=(c == DC - 1))
                last.then_inc(tile_done, 1)
            project("memk", chunk(B3), is_normed("mem"))
            values("memv", B3, 2)
            project("q", chunk(H), is_normed("mix"))
            project("k", chunk(H), is_normed("mix"))
            values("v", H, 1)

            v1 = B5[:, 0:4, :].rearrange("p c t -> p (c t)").rearrange("p (t d) -> p t d", t=TT)
            memv = B2[:, :, :].rearrange("p c t -> p (c t)").rearrange("p (t d) -> p t d", t=TT)
            keyside = const("keyside").rearrange("p (j t) -> p j t", j=4)
            queryside = const("queryside")
            pe.wait_ge(taken["act"], plan.stage["v"][1].emptied)
            pe.wait_ge(bias_ready, 1)
            for s in range(HEADS + 2):
                if s < HEADS:
                    c, r0 = s // 2, (s % 2) * DH
                    if s >= 2:
                        pe.wait_ge(score_read, s - 1)
                    for qt in range(TT):
                        o = bank(4 + s % 2)[:, qt * P:qt * P + P + qt * P]
                        keys = (qt + 1) * P
                        pe.matmul(o, B4[r0:r0 + DH, c, qt * P:(qt + 1) * P], B4[r0:r0 + DH, 4 + c, 0:keys], start=True, stop=False)
                        last = pe.matmul(o, queryside[r0:r0 + 40, qt * P:(qt + 1) * P], keyside[r0:r0 + 40, c, 0:keys], start=False, stop=True)
                    last.then_inc(score_done, 1)
                if 1 <= s <= HEADS:
                    h = s - 1
                    pe.wait_ge(prob_ready, TT * h + 2)
                    if h:
                        pe.wait_ge(turned_copied, h)
                    p_ = work[:, h % 2, :]
                    pe.transpose(bank(6)[:, 0:P], p_[:, 0:P], ident)
                    pe.transpose(bank(6)[:, P:2 * P], p_[:, P:2 * P], ident)
                    pe.transpose(bank(6)[:, 2 * P:3 * P], p_[:, 2 * P:3 * P], ident).then_inc(turned, 1)
                if s >= 2:
                    h = s - 2
                    r0 = (h % 2) * DH
                    pe.wait_ge(turned_copied, h + 1)
                    if h % 2 == 0 and h:
                        pe.wait_ge(o_copied, h // 2)
                    o = bank(7)[r0:r0 + DH, 0:T]
                    pt = work[:, 2 + h % 2, :]
                    pe.matmul(o, v1[:, 0, h * DH:(h + 1) * DH], pt[:, 0:T], start=True, stop=False)
                    last = pe.matmul(bank(7)[r0:r0 + DH, P:T], v1[:, 1, h * DH:(h + 1) * DH], pt[:, T:T + P], start=False, stop=True)
                    if h % 2:
                        last.then_inc(o_done, 1)
            norm("attn")
            for c in range(AC):
                pe.wait_ge(conv_step, 4 * (TAPS - 1) + c + 1)
                last = pe.matmul(bank(5)[:, 0:T], ones, B5[:, 4 + c, :], start=(c == 0), stop=(c == AC - 1))
            last.then_inc(mean_done, 1)
            norm("conv")

            def mixed(c):
                if c < AC:
                    pe.wait_ge(normed, NORM["attn"][2] + c + 1)
                else:
                    pe.wait_ge(conv_out, c - AC + 1)

            project("wout", chunk(B6), mixed)
            norm("memq")
            project("mq", chunk(H), is_normed("memq"))
            pe.wait_ge(taken["act"], plan.stage["mq"][7].emptied)
            for s in range(MH + 2):
                g = HEADS + s
                if s < MH:
                    if s >= 2:
                        pe.wait_ge(exp_done, TT * (g - 1))
                    for qt in range(TT):
                        for c in range(2):
                            last = pe.matmul(bank(4 + g % 2)[:, qt * T:(qt + 1) * T], B4[:, 2 * s + c, qt * P:(qt + 1) * P],
                                             B1[:, 2 * s + c, :], start=(c == 0), stop=(c == 1))
                    last.then_inc(score_done, 1)
                if 1 <= s <= MH:
                    h = g - 1
                    pe.wait_ge(prob_ready, TT * h + 2)
                    pe.wait_ge(turned_copied, h)
                    for qt in range(TT):
                        for kt in range(TT):
                            last = pe.transpose(bank(6)[:, kt * T + qt * P:kt * T + (qt + 1) * P],
                                                work[:, h % 2, qt * T + kt * P:qt * T + (kt + 1) * P], ident)
                    last.then_inc(turned, 1)
                if s >= 2:
                    h = g - 2
                    pe.wait_ge(turned_copied, h + 1)
                    pe.wait_ge(o_copied, HEADS // 2 + s - 2)
                    for c in range(2):
                        for kt in range(TT):
                            f0 = (2 * (s - 2) + c) * P
                            last = pe.matmul(bank(7)[:, c * T:(c + 1) * T], memv[:, kt, f0:f0 + P],
                                             work[:, 2 + h % 2, kt * T:(kt + 1) * T], start=(kt == 0), stop=(kt == 1))
                    last.then_inc(o_done, 1)
            project("mo", chunk(B5), lambda c: pe.wait_ge(o_copied, HEADS // 2 + c // 2 + 1))
            norm("moe")
            for m, t in enumerate(plan.stage["htok"]):
                open_tile(t)
                for c in range(4):
                    pe.wait_ge(normed, NORM["moe"][2] + (m % 2) * 4 + c + 1)
                    last = pe.transpose(bank(t.bank)[:, c * P:(c + 1) * P], H[:, (m % 2) * 4 + c, (m // 2) * P:(m // 2 + 1) * P], ident)
                last.then_inc(tile_done, 1)
            t = plan.stage["route"][0]
            open_tile(t)
            pe.wait_ge(inputs_loaded[5], 16)
            for tt in range(TT):
                for c in range(DC):
                    last = pe.matmul(bank(t.bank)[:, tt * NL:(tt + 1) * NL], H[:, c, tt * P:(tt + 1) * P], wr[:, c, :],
                                     start=(c == 0), stop=(c == DC - 1))
            last.then_inc(tile_done, 1)
            t = plan.stage["rank"][0]
            open_tile(t)
            pe.wait_ge(chosen_ready, 1)
            pe.matmul(bank(t.bank)[:, 0:E], const("before"), chosen[:, 0, :], start=True, stop=True)
            pe.matmul(bank(t.bank)[:, E:2 * E], const("before"), chosen[:, 1, :], start=True, stop=False)
            pe.matmul(bank(t.bank)[:, E:2 * E], ones, chosen[:, 0, :], start=False, stop=True).then_inc(tile_done, 1)
            t = plan.stage["maxrank"][0]
            open_tile(t)
            pe.wait_ge(maxrank_in, 1)
            pe.transpose(bank(t.bank)[0:1, 0:P], mr[:, 0:1], ident).then_inc(tile_done, 1)

            def gather(S, k):
                pe.wait_ge(S.disp_ready, 2 * k + 1)
                for b in range(2):
                    for c in range(4):
                        for tt in range(TT):
                            f0 = (4 * b + c) * P
                            last = pe.matmul(bank(1 + 2 * b)[:, c * P:(c + 1) * P], htok[:, tt, f0:f0 + P],
                                             disp[:, tt, :, :].rearrange("p e s -> p (e s)"), start=(tt == 0), stop=(tt == TT - 1))
                    last.then_inc(S.gathered, 1)

            def turn_back(S, k):
                pe.wait_ge(S.disp_ready, 2 * k + 2)
                for tt in range(TT):
                    last = pe.transpose(bank(2)[:, tt * P:(tt + 1) * P], comb[:, tt, :, :].rearrange("p e s -> p (e s)"), ident)
                last.then_inc(S.comb_turned, 1)

            def hidden(S, k, landed):
                pe.wait_ge(S.xg_ready, 2 * k + 2)
                for g, slots in enumerate([(S_G0, S_G1), (S_U0, S_U1)]):
                    for s in slots:
                        landed(s)
                    for c in range(DC):
                        for e, s in enumerate(slots):
                            w = ring[:, s, :].rearrange("p (c n) -> p c n", c=DC)
                            last = pe.matmul(bank(3 + g)[e * CAP:(e + 1) * CAP, :], XG[:, c, e * CAP:(e + 1) * CAP], w[:, c, :],
                                             start=(c == 0), stop=(c == DC - 1))
                    last.then_inc(S.hidden_done, 1)

            def turn_hidden(S, k):
                pe.wait_ge(S.eprod_ready, k + 1)
                for f in range(FEC):
                    last = pe.transpose(bank(0)[:, f * P:(f + 1) * P], eprod[:, f * P:(f + 1) * P], ident)
                last.then_inc(S.hidden_turned, 1)

            def down(S, k, landed):
                for s in (S_D0, S_D1):
                    landed(s)
                pe.wait_ge(S.ehid_ready, k + 1)
                for b in range(2):
                    for f in range(FEC):
                        for e, s in enumerate((S_D0, S_D1)):
                            w = ring[:, s, :].rearrange("p (f n) -> p f n", f=FEC)
                            last = pe.matmul(bank(5 + b)[e * CAP:(e + 1) * CAP, :], ehid[:, f, e * CAP:(e + 1) * CAP],
                                             w[:, f, b * 512:(b + 1) * 512], start=(f == 0), stop=(f == FEC - 1))
                    last.then_inc(S.y_done, 1)

            def spread(S, k, y_value, back_value):
                pe.wait_ge(S.y_ready, y_value)
                pe.wait_ge(S.back_ready, back_value)
                for r in range(4):
                    if r >= 2:
                        pe.wait_ge(S.spread_taken, 4 * k + r - 1)
                    b = 7 if r % 2 == 0 else 2
                    for j in range(2):
                        c = 2 * r + j
                        last = pe.matmul(bank(b)[:, j * T:(j + 1) * T], Y[:, c * P:(c + 1) * P], back[:, :], start=True, stop=True)
                    last.then_inc(S.spread_done, 1)

            pe.wait_ge(taken["act"], plan.stage["htok"][3].emptied)
            wait_taken(pe, plan.stage["maxrank"][0])
            gather(hot, 0)
            with pe.Fori(0, PAIRS) as n:
                def landed(s):
                    pe.wait_ge(loaded[s], 16 * n + MOE_BASE[s] + 16)

                hidden(hot, n, landed)
                spread(hot, n, 2 * n + 1, n + 1)
                turn_hidden(hot, n)
                gather(hot, n + 1)
                pe.wait_ge(hot.spread_taken, 4 * n + 4)
                turn_back(hot, n)
                down(hot, n, landed)
            spread(hot, PAIRS, 2 * PAIRS + 1, PAIRS + 1)
            pe.wait_ge(npass_ready, 1)
            passes = pe.value_load(npass[0:1, 0:1], min_val=1, max_val=4)
            with pe.If(passes > 1):
                pe.wait_ge(hot.spread_taken, 4 * (PAIRS + 1))
                pe.wait_ge(hot.xg_ready, 2 * (PAIRS + 1))
                with pe.Fori(1, passes) as q:
                    with pe.Fori(0, PAIRS) as n:
                        k = (q - 1) * PAIRS + n

                        def landed(s):
                            pe.wait_ge(cold_loaded, 96 * k + 96)

                        gather(cold, k)
                        turn_back(cold, k)
                        hidden(cold, k, landed)
                        turn_hidden(cold, k)
                        down(cold, k, landed)
                        spread(cold, k, 2 * k + 2, k + 1)
                        pe.wait_ge(cold.spread_taken, 4 * k + 4)
                        pe.nop()
            norm("final")

            def swiglu(which):
                base = plan.first[f"ffn{which}"]
                tiles = plan.stage[f"ffn{which}"]

                def gate_up(j, i=0, looped=False):
                    n = base + j
                    pe.wait_ge(loaded[n % SLOTS], 16 * i + plan.pieces[n][4] if looped else plan.pieces[n][4])
                    w = ring[:, n % SLOTS, 0:2 * D].rearrange("p (c g m) -> p c g m", c=DC, g=2)
                    for g in range(2):
                        for c in range(DC):
                            if j == 0 and g == 0:
                                pe.wait_ge(normed, NORM[f"ffn{which}"][2] + c + 1)
                            last = pe.matmul(bank(4 + j % 2)[:, g * T:(g + 1) * T], w[:, c, g, :], H[:, c, :],
                                             start=(c == 0), stop=(c == DC - 1))
                    last.then_inc(gu_done, 1)

                def down_of(j, hidden_value, first=False, final=False):
                    n = base + j
                    pe.wait_ge(hid_ready, hidden_value)
                    w = ring[:, n % SLOTS, 2 * D:3 * D]
                    for m in range(DC):
                        if first and m % 2 == 0:
                            open_tile(tiles[m // 2])
                        last = pe.matmul(bank(m // 2)[:, (m % 2) * T:(m % 2 + 1) * T], w[:, m * P:(m + 1) * P], hid[:, j % 3, :],
                                         start=(first and m % 2 == 0), stop=final, skip_group_check=True)
                        if final and m % 2:
                            last.then_inc(tile_done, 1)
                    if not final:
                        last.then_inc(down_done, 1)

                gate_up(0)
                gate_up(1)
                down_of(0, FC * which + 1, first=True)
                with pe.Fori(0, 3) as i:
                    for j in range(2, 8):
                        gate_up(j, i, looped=True)
                        down_of(j - 1, 6 * i + FC * which + j)
                for j in range(20, FC):
                    gate_up(j)
                    down_of(j - 1, FC * which + j)
                down_of(FC - 1, FC * which + FC, final=True)

            norm("ffn0")
            swiglu(0)
            norm("lru")
            project("rec", chunk(H), is_normed("lru"))
            project("gate", chunk(H), is_normed("lru"))
            wait_piece(pe, "r", 0)
            w = ring[:, slot_of("r", 0), :].rearrange("p (g n k m) -> p g n k m", g=2, n=NB, k=2)
            for g, stage in enumerate(["r", "i"]):
                for m, t in enumerate(plan.stage[stage]):
                    open_tile(t)
                    for k in range(2):
                        pe.wait_ge(xconv_ready, 2 * (m // 2) + k + 1)
                        last = pe.matmul(bank(t.bank)[:, 0:T], w[:, g, m // 2, k, (m % 2) * P:(m % 2 + 1) * P], B1[:, 2 * (m // 2) + k, :],
                                         start=(k == 0), stop=(k == 1))
                    last.then_inc(tile_done, 1)
            project("aout", chunk(H), lambda c: pe.wait_ge(lru_out, c + 1))
            norm("ffn1")
            swiglu(1)
            norm("kv")

            def project_heads(stage, base, name):
                def headsum(m):
                    pe.wait_ge(taken["act"], plan.stage[stage][m].emptied)
                    if base + m >= 2:
                        pe.wait_ge(headroot, base + m - 1)
                    pe.matmul(bank(4 + m % 2)[:, 0:T], const("headsum"), work[:, m % 2, 0:T], start=True, stop=True).then_inc(headsum_done, 1)

                for m, t in enumerate(plan.stage[stage]):
                    if m % 4 == 0:
                        wait_piece(pe, stage, m // 4)
                    open_tile(t)
                    w = piece(stage, m // 4, DC)
                    for c in range(DC):
                        if m == 0:
                            pe.wait_ge(normed, NORM[name][2] + c + 1)
                        last = pe.matmul(bank(t.bank)[:, 0:T], w[:, c, (m % 4) * P:(m % 4 + 1) * P], H[:, c, :],
                                         start=(c == 0), stop=(c == DC - 1))
                    last.then_inc(tile_done, 1)
                    if m:
                        headsum(m - 1)
                headsum(7)

            project_heads("kvk", 0, "kv")
            values("kvv", H, 2)
            norm("ffn2")
            swiglu(2)
            norm("stick")
            project_heads("bq", 8, "stick")

            pe.wait_ge(head_ready, 16)
            for s in range(SH + 2):
                if s < SH:
                    c, r0 = s // 2, (s % 2) * DH
                    if s >= 2:
                        pe.wait_ge(log1p_ready, 2 * (s - 1))
                    pe.matmul(bank(4 + s % 2)[:, 0:T], B1[r0:r0 + DH, c, 0:P], B3[r0:r0 + DH, c, :], start=True, stop=True)
                    pe.matmul(bank(4 + s % 2)[:, T:T + P], B1[r0:r0 + DH, c, P:T], B3[r0:r0 + DH, c, P:T], start=True, stop=True).then_inc(z_done, 1)
                if 1 <= s <= SH:
                    h = s - 1
                    pe.wait_ge(stay_in, h + 1)
                    if h:
                        pe.wait_ge(logw_ready, h)
                    ls = B6[:, 2 * (h % 2):2 * (h % 2) + 2, :].rearrange("p c t -> p (c t)")
                    pe.matmul(bank(6)[:, 0:T], const("after"), ls[:, 0:T], start=True, stop=False)
                    pe.matmul(bank(6)[:, P:T], ones, ls[:, T:T + P], start=False, stop=True)
                    pe.matmul(bank(6)[:, T:T + P], const("after"), ls[:, T:T + P], start=True, stop=True).then_inc(stay_done, 1)
                if s >= 2:
                    h = s - 2
                    r0 = (h % 2) * DH
                    pe.wait_ge(w_ready, h + 1)
                    if h % 2 == 0 and h:
                        pe.wait_ge(so_copied, h // 2)
                    w = B5[:, 4 + 2 * (h % 2):6 + 2 * (h % 2), :].rearrange("p c t -> p (c t)")
                    pe.matmul(bank(7)[r0:r0 + DH, 0:T], memv[:, 0, h * DH:(h + 1) * DH], w[:, 0:T], start=True, stop=False)
                    last = pe.matmul(bank(7)[r0:r0 + DH, P:T], memv[:, 1, h * DH:(h + 1) * DH], w[:, T:T + P], start=False, stop=True)
                    last.then_inc(so_done, 1)
            project("bo", chunk(B4), lambda c: pe.wait_ge(so_copied, c + 1))
            norm("ffn3")
            swiglu(3)

        @block.vector
        def _(dve):
            steps = [0]

            def step(ins):
                ins.then_inc(vstep, 1)
                steps[0] += 1
                dve.wait_ge(vstep, steps[0])

            def norm(name, src, dst, gain, width=D):
                n, chunks, base = NORM[name]
                dve.wait_ge(msum_done, n + 1)
                if n:
                    dve.wait_ge(rs_ready, n)
                dve.tensor_scalar(ms[:, :], bank(6)[:, 0:TT], 1.0 / width, EPS, ALU.mult, ALU.add).then_inc(ms_ready, 1)
                dve.wait_ge(rs_ready, n + 1)
                if n:
                    dve.wait_ge(rbcast_done, n)
                for t in range(TT):
                    dve.tensor_scalar(diag[:, t * P:(t + 1) * P], ident, rs[:, t:t + 1], None, ALU.mult).then_inc(diag_ready, 1)
                dve.wait_ge(rbcast_done, n + 1)
                for c in range(chunks):
                    dve.scalar_tensor_tensor(out=dst(c), in0=src(c), scalar=gain(c), in1=bank(7)[:, 0:T],
                                             op0=ALU.mult, op1=ALU.mult).then_inc(normed, 1)

            def chunk(buf, first=0):
                return lambda c: buf[:, first + c, :]

            def gain(name):
                return lambda c: vec(name, c)

            def add_tile(stage, m):
                t = plan.stage[stage][m]
                dve.wait_ge(tile_done, t.n + 1)
                dve.tensor_tensor(X[:, m, :], bank(t.bank)[:, 0:T], X[:, m, :], ALU.add).then_inc(taken["dve"], 1)

            dve.wait_ge(inputs_loaded[0], 16)
            dve.wait_ge(inputs_loaded[1], 16)
            dve.wait_ge(inputs_loaded[3], 16)
            norm("mem", chunk(B3), chunk(B3), gain("mem_norm"))
            dve.wait_ge(inputs_loaded[2], 16)
            norm("mix", chunk(X), chunk(H), gain("norm_mix"))
            t = plan.stage["forget"][0]
            dve.wait_ge(tile_done, t.n + 1)
            dve.tensor_scalar(small[0:HEADS, 0, :], bank(t.bank)[0:HEADS, 0:T], vec("b_forget")[0:HEADS, :], None, ALU.add).then_inc(taken["dve"], 1)
            dve.wait_ge(forget_exp, 1)
            step(dve.scalar_tensor_tensor(out=small[0:HEADS, 3, :], in0=small[0:HEADS, 0, :], scalar=0.0, in1=small[0:HEADS, 2, :],
                                          op0=ALU.min, op1=ALU.subtract))
            queryside = const("queryside")
            step(dve.tensor_tensor_scan(queryside[0:HEADS, :], const("scan1")[0:HEADS, :], small[0:HEADS, 3, :], 0.0, ALU.mult, ALU.add))
            dve.tensor_copy(queryside[DH:DH + HEADS, :], queryside[0:HEADS, :]).then_inc(vstep, 1)
            keyside = const("keyside").rearrange("p (j t) -> p j t", j=4)
            pick = const("pick").rearrange("p (a j) -> p a j", a=2)
            for a in range(2):
                for j in range(4):
                    r0 = a * DH + 32
                    last = dve.tensor_scalar(keyside[r0:r0 + HEADS, j, :], queryside[0:HEADS, :], pick[0:HEADS, a, j:j + 1], None, ALU.mult)
                    last.then_inc(bias_ready if (a, j) == (1, 3) else vstep, 1)
            steps[0] += 8
            at = VECTORS["lam"][0]
            dve.wait_ge(lam_ready, 1)
            step(dve.tensor_scalar(spl[:, 2, :], V[:, at:at + DC], -1.0, 0.0, ALU.mult, ALU.max))
            step(dve.tensor_tensor(spl[:, 2, :], spl[:, 2, :], spl[:, 1, :], ALU.add))
            dve.tensor_scalar(spl[:, 3, :], spl[:, 2, :], -8.0, None, ALU.mult).then_inc(lam_ready, 1)
            step(dve.tensor_scalar(qg[:, :], vec("q_gain"), DH ** -0.5, None, ALU.mult))
            dve.wait_ge(prepared, 1)
            for c in range(AC):
                dve.wait_ge(taken["act"], plan.stage["glu"][2 * c].emptied)
                t = plan.stage["glu"][2 * c + 1]
                dve.wait_ge(tile_done, t.n + 1)
                dve.scalar_tensor_tensor(out=zin[:, c, PAD:PAD + T], in0=bank(t.bank)[:, 0:T], scalar=vec("b_glu", c), in1=B6[:, 4 + c, :],
                                         op0=ALU.add, op1=ALU.mult).then_inc(taken["dve"], 1)
            dve.wait_ge(taken["dve"], plan.stage["glu"][7].emptied)
            for k in range(TAPS):
                for c in range(AC):
                    z = zin[:, c, PAD - TAPS + 1 + k:PAD - TAPS + 1 + k + T]
                    if k == 0:
                        ins = dve.tensor_scalar(B5[:, 4 + c, :], z, vec("w_dw", 4 * k + c), vec("b_dw", c), ALU.mult, ALU.add)
                    else:
                        dve.wait_ge(conv_step, 4 * k + c - 3)
                        ins = dve.scalar_tensor_tensor(out=B5[:, 4 + c, :], in0=z, scalar=vec("w_dw", 4 * k + c), in1=B5[:, 4 + c, :],
                                                       op0=ALU.mult, op1=ALU.add)
                    ins.then_inc(conv_step, 1)

            def softmax_scale(g, widths):
                dve.wait_ge(exp_done, TT * (g + 1))
                step(dve.reciprocal(rowinv[:, g % 2, :], rowsum[:, g % 2, :]))
                at = 0
                for t, w in enumerate(widths):
                    dve.tensor_scalar(work[:, g % 2, at:at + w], work[:, g % 2, at:at + w], rowinv[:, g % 2, t:t + 1], None, ALU.mult).then_inc(prob_ready, 1)
                    at += w

            for s in range(HEADS + 1):
                if s < HEADS:
                    dve.wait_ge(score_done, s + 1)
                    if s >= 2:
                        dve.wait_ge(turned, s - 1)
                    dve.tensor_tensor(work[:, s % 2, 0:3 * P], bank(4 + s % 2)[:, 0:3 * P], const("causal"), ALU.add).then_inc(score_read, 1)
                    dve.wait_ge(score_read, s + 1)
                    step(dve.tensor_reduce(negmax[:, s % 2, 0:1], work[:, s % 2, 0:P], AX.X, ALU.max, negate=True))
                    dve.tensor_reduce(negmax[:, s % 2, 1:2], work[:, s % 2, P:3 * P], AX.X, ALU.max, negate=True).then_inc(max_ready, 1)
                if s >= 1:
                    softmax_scale(s - 1, [P, T])
            norm("attn", chunk(B3), chunk(B6), gain("attn_g"), width=DA)
            dve.wait_ge(mean_done, 1)
            for c in range(AC):
                dve.scalar_tensor_tensor(out=B5[:, 4 + c, :], in0=bank(5)[:, 0:T], scalar=-1.0 / DA, in1=B5[:, 4 + c, :],
                                         op0=ALU.mult, op1=ALU.add).then_inc(centred, 1)
            norm("conv", chunk(B5, 4), chunk(B6, 4), gain("ln_g"), width=DA)
            for m in range(8):
                add_tile("wout", m)
            norm("memq", chunk(X), chunk(H), gain("norm_mem"))
            for s in range(MH + 1):
                g = HEADS + s
                if s < MH:
                    dve.wait_ge(score_done, g + 1)
                    dve.tensor_reduce(negmax[:, g % 2, :], bank(4 + g % 2).rearrange("p (t k) -> p t k", t=TT), AX.X, ALU.max,
                                      negate=True).then_inc(max_ready, 1)
                if s >= 1:
                    softmax_scale(g - 1, [T, T])
            for m in range(8):
                add_tile("mo", m)
            norm("moe", chunk(X), chunk(H), gain("norm_ffn"))

            t = plan.stage["route"][0]
            dve.wait_ge(tile_done, t.n + 1)
            at = VECTORS["b_route"][0]
            dve.tensor_tensor(lg[:, :, :], bank(t.bank)[:, 0:TT * NL].rearrange("p (t n) -> p t n", t=TT),
                              V[:, at:at + NL].unsqueeze(1).to_broadcast([P, TT, NL]), ALU.add).then_inc(taken["dve"], 1)
            dve.wait_ge(taken["dve"], t.emptied)

            def over(ap, n):
                return ap.unsqueeze(2).to_broadcast([P, TT, n])

            def first(name, n):
                return const(name).unsqueeze(1).to_broadcast([P, TT, n])

            def top1(dist, n, name, score, best, onehot):
                step(dve.tensor_scalar(score, dist, 0.0, None, ALU.is_ge))
                step(dve.tensor_tensor(score, score, first(name, n), ALU.mult))
                step(dve.tensor_reduce(best, score, AX.X, ALU.max))
                step(dve.tensor_tensor(onehot, score, over(best, n), ALU.is_equal))

            step(dve.tensor_reduce(r1[:, 0, :], lg[:, :, 0:GROUPS], AX.X, ALU.max))
            dve.tensor_tensor(r4[:, 0, :, :], lg[:, :, 0:GROUPS], over(r1[:, 0, :], GROUPS), ALU.subtract).then_inc(router_in, 1)
            dve.wait_ge(router_in, 1)
            gsel = r4[:, 3, :, :]
            top1(r4[:, 0, :, :], GROUPS, "first4", r4[:, 2, :, :], r1[:, 1, :], gsel)
            step(dve.tensor_tensor(pick32[:, :, :, :].rearrange("p t j g -> p t g j"),
                                   lg[:, :, GROUPS:NL].rearrange("p t (g j) -> p t g j", g=GROUPS),
                                   gsel.unsqueeze(3).to_broadcast([P, TT, GROUPS, PER]), ALU.mult))
            step(dve.tensor_reduce(r8[:, 0, :, :], pick32[:, :, :, :], AX.X, ALU.add))
            step(dve.tensor_reduce(r1[:, 3, :], r8[:, 0, :, :], AX.X, ALU.max))
            step(dve.tensor_tensor(r8[:, 1, :, :], r8[:, 0, :, :], over(r1[:, 3, :], PER), ALU.subtract))
            oh1, oh2 = r8[:, 3, :, :], r8[:, 6, :, :]
            top1(r8[:, 1, :, :], PER, "first8", r8[:, 2, :, :], r1[:, 4, :], oh1)
            step(dve.scalar_tensor_tensor(out=r8[:, 4, :, :], in0=oh1, scalar=-BIG, in1=r8[:, 1, :, :], op0=ALU.mult, op1=ALU.add))
            dve.tensor_reduce(r1[:, 5, :], r8[:, 4, :, :], AX.X, ALU.max).then_inc(router_in, 1)
            dve.wait_ge(router_in, 2)
            step(dve.tensor_tensor(r8[:, 5, :, :], r8[:, 4, :, :], over(r1[:, 5, :], PER), ALU.subtract))
            top1(r8[:, 5, :, :], PER, "first8", r8[:, 2, :, :], r1[:, 4, :], oh2)
            step(dve.tensor_tensor(r8[:, 7, :, :], oh1, oh2, ALU.add))
            dve.tensor_tensor(chosen[:, :, :].rearrange("p t (g j) -> p t g j", g=GROUPS),
                              gsel.unsqueeze(3).to_broadcast([P, TT, GROUPS, PER]),
                              r8[:, 7, :, :].unsqueeze(2).to_broadcast([P, TT, GROUPS, PER]), ALU.mult).then_inc(chosen_ready, 1)
            dve.wait_ge(router_exp, 2)
            step(dve.tensor_reduce(r1[:, 2, :], r4[:, 1, :, :], AX.X, ALU.add))
            step(dve.tensor_scalar(r1[:, 7, :], r1[:, 6, :], 1.0, None, ALU.add))
            step(dve.tensor_tensor(r1[:, 7, :], r1[:, 7, :], r1[:, 2, :], ALU.mult))
            step(dve.reciprocal(r1[:, 8, :], r1[:, 7, :]))
            step(dve.tensor_tensor(r1[:, 9, :], r1[:, 8, :], r1[:, 6, :], ALU.mult))
            step(dve.tensor_tensor(r8[:, 0, :, :], oh1, over(r1[:, 8, :], PER), ALU.mult))
            step(dve.tensor_tensor(r8[:, 1, :, :], oh2, over(r1[:, 9, :], PER), ALU.mult))
            step(dve.tensor_tensor(r8[:, 0, :, :], r8[:, 0, :, :], r8[:, 1, :, :], ALU.add))
            dve.wait_ge(prepared, 3)
            step(dve.tensor_tensor(gates[:, :, 0:E].rearrange("p t (g j) -> p t g j", g=GROUPS),
                                   gsel.unsqueeze(3).to_broadcast([P, TT, GROUPS, PER]),
                                   r8[:, 0, :, :].unsqueeze(2).to_broadcast([P, TT, GROUPS, PER]), ALU.mult))
            t = plan.stage["rank"][0]
            dve.wait_ge(tile_done, t.n + 1)
            dve.wait_ge(chosen_ready, 1)
            dve.scalar_tensor_tensor(out=rank[:, :, 0:E], in0=bank(t.bank)[:, 0:TT * E].rearrange("p (t e) -> p t e", t=TT), scalar=1.0,
                                     in1=chosen[:, :, :], op0=ALU.add, op1=ALU.mult).then_inc(taken["dve"], 1)
            dve.wait_ge(taken["dve"], t.emptied)
            step(dve.tensor_scalar(rank[:, :, 0:E], rank[:, :, 0:E], -1.0, None, ALU.add))
            dve.tensor_reduce(mr[:, 0:1], rank[:, :, :].rearrange("p t e -> p (t e)"), AX.X, ALU.max).then_inc(maxrank_in, 1)
            t = plan.stage["maxrank"][0]
            dve.wait_ge(tile_done, t.n + 1)
            dve.tensor_reduce(mrow[0:1, 0:1], bank(t.bank)[0:1, 0:P], AX.X, ALU.max).then_inc(taken["dve"], 1)
            dve.wait_ge(taken["dve"], t.emptied)
            step(dve.tensor_scalar(mrow[0:1, 4:8], const("passes")[0:1, :], mrow[0:1, 0:1], None, ALU.is_le))
            step(dve.tensor_reduce(mrow[0:1, 1:2], mrow[0:1, 4:8], AX.X, ALU.add))
            dve.tensor_copy(npass[:, :], mrow[0:1, 1:2]).then_inc(npass_ready, 1)

            slots = const("slots").unsqueeze(1).unsqueeze(1).to_broadcast([P, TT, 2, CAP])

            def dispatch(S, k, n):
                dve.tensor_tensor(disp[:, :, :, :], slots, rank[:, :, bass.ds(2 * n, 2)].unsqueeze(3).to_broadcast([P, TT, 2, CAP]),
                                  ALU.is_equal).then_inc(S.disp_ready, 1)

            def combine(S, k, n):
                dve.wait_ge(S.disp_ready, 2 * k + 1)
                dve.tensor_tensor(comb[:, :, :, :], disp[:, :, :, :],
                                  gates[:, :, bass.ds(2 * n, 2)].unsqueeze(3).to_broadcast([P, TT, 2, CAP]), ALU.mult).then_inc(S.disp_ready, 1)

            def expert_hidden(S, k):
                dve.wait_ge(S.esilu_ready, k + 1)
                dve.wait_ge(S.hidden_done, 2 * k + 2)
                dve.tensor_tensor(eprod, esilu, bank(4), ALU.mult).then_inc(S.eprod_ready, 1)

            def collect(S, k):
                for r in range(4):
                    dve.wait_ge(S.spread_done, 4 * k + r + 1)
                    xs = X[:, 2 * r:2 * r + 2, :].rearrange("p c t -> p (c t)")
                    dve.tensor_tensor(xs, bank(7 if r % 2 == 0 else 2), xs, ALU.add).then_inc(S.spread_taken, 1)

            dve.memset(Y, 0.0).then_inc(vstep, 1)
            dve.memset(back, 0.0).then_inc(vstep, 1)
            steps[0] += 2
            dispatch(hot, 0, 0)
            combine(hot, 0, 0)
            dve.wait_ge(hot.gathered, 2)
            dve.wait_ge(hot.disp_ready, 2)
            dispatch(hot, 1, 1)
            with dve.Fori(0, PAIRS) as n:
                expert_hidden(hot, n)
                collect(hot, n)
                dve.wait_ge(hot.comb_turned, n + 1)
                combine(hot, n + 1, n + 1)
                dve.wait_ge(hot.gathered, 2 * n + 4)
                dve.wait_ge(hot.disp_ready, 2 * n + 4)
                dispatch(hot, n + 2, n + 2)
            collect(hot, PAIRS)
            dve.wait_ge(hot.spread_taken, 4 * PAIRS + 4)
            dve.wait_ge(npass_ready, 1)
            passes = dve.value_load(npass[0:1, 0:1], min_val=1, max_val=4)
            with dve.If(passes > 1):
                dve.wait_ge(hot.disp_ready, 2 * PAIRS + 3)
                with dve.Fori(1, passes) as q:
                    dve.tensor_scalar(rank[:, :, :], rank[:, :, :], -float(CAP), None, ALU.add).then_inc(shifted, 1)
                    with dve.Fori(0, PAIRS) as n:
                        k = (q - 1) * PAIRS + n
                        dve.wait_ge(shifted, q)
                        dispatch(cold, k, n)
                        combine(cold, k, n)
                        expert_hidden(cold, k)
                        collect(cold, k)
                        dve.wait_ge(cold.gathered, 2 * k + 2)
                        dve.wait_ge(cold.comb_turned, k + 1)
                        dve.wait_ge(cold.disp_ready, 2 * k + 2)
                        dve.wait_ge(cold.spread_taken, 4 * k + 4)
            dve.nop().then_inc(chosen_ready, 1)
            norm("final", chunk(X), chunk(X), gain("final"))

            def swiglu(which):
                base = FC * which

                def one(j, i=0):
                    dve.wait_ge(ffn_silu, base + j + 1 + i)
                    if j >= 3 or not isinstance(i, int):
                        dve.wait_ge(down_done, (FC - 1) * which + j - 1 + i)
                    dve.tensor_tensor(hid[:, j % 3, :], act2[:, j % 2, :], bank(4 + j % 2)[:, T:2 * T], ALU.mult).then_inc(hid_ready, 1)

                for j in range(2):
                    one(j)
                with dve.Fori(0, 3) as i:
                    for j in range(2, 8):
                        one(j, 6 * i)
                for j in range(20, FC):
                    one(j)
                for b, t in enumerate(plan.stage[f"ffn{which}"]):
                    dve.wait_ge(tile_done, t.n + 1)
                    xs = X[:, 2 * b:2 * b + 2, :].rearrange("p c t -> p (c t)")
                    dve.scalar_tensor_tensor(out=xs, in0=bank(b), scalar=0.5, in1=xs, op0=ALU.mult, op1=ALU.add).then_inc(taken["dve"], 1)

            norm("ffn0", chunk(X), chunk(H), gain("ffn1_0"))
            swiglu(0)
            norm("lru", chunk(X), chunk(H), gain("mix_0"))
            for m in range(8):
                wait_taken(dve, plan.stage["rec"][m])
                for k in range(TAPS2):
                    z = zin[:, m, PAD - TAPS2 + 1 + k:PAD - TAPS2 + 1 + k + T]
                    if k == 0:
                        step(dve.tensor_scalar(B1[:, m, :], z, vec("conv_w", 8 * k + m), vec("conv_b", m), ALU.mult, ALU.add))
                    else:
                        ins = dve.scalar_tensor_tensor(out=B1[:, m, :], in0=z, scalar=vec("conv_w", 8 * k + m), in1=B1[:, m, :],
                                                       op0=ALU.mult, op1=ALU.add)
                        if k < TAPS2 - 1:
                            step(ins)
                        else:
                            ins.then_inc(xconv_ready, 1)
            for m in range(8):
                wait_taken(dve, plan.stage["i"][m])
                dve.wait_ge(xconv_ready, m + 1)
                step(dve.tensor_tensor(B4[:, m, :], B4[:, m, :], B1[:, m, :], ALU.mult))
            for m in range(8):
                dve.wait_ge(decay_ready, 2 * m + 2)
                step(dve.tensor_tensor(SQ[:, m, :], B5[:, m, :], B5[:, m, :], ALU.mult))
                dve.scalar_tensor_tensor(out=B6[:, m, :], in0=SQ[:, m, :], scalar=1.0, in1=B6[:, m, :],
                                         op0=ALU.add, op1=ALU.mult).then_inc(ssq_ready, 1)
            for m in range(8):
                dve.wait_ge(root_ready, m + 1)
                step(dve.tensor_tensor(B4[:, m, :], B4[:, m, :], B6[:, m, :], ALU.mult))
                step(dve.tensor_tensor_scan(B3[:, m, :], B5[:, m, :], B4[:, m, :], 0.0, ALU.mult, ALU.add))
                dve.tensor_tensor(H[:, m, :], B3[:, m, :], B2[:, m, :], ALU.mult).then_inc(lru_out, 1)
            for m in range(8):
                add_tile("aout", m)
            norm("ffn1", chunk(X), chunk(H), gain("ffn2_0"))
            swiglu(1)
            norm("kv", chunk(X), chunk(H), gain("kv"))

            def head_norm(dst, base, g):
                for m in range(8):
                    dve.wait_ge(headroot, base + m + 1)
                    dve.wait_ge(headsq, base + m + 1)
                    r = work[:, 4 + m % 2, 0:T]
                    step(dve.reciprocal(r, work[:, 2 + m % 2, 0:T]))
                    dve.scalar_tensor_tensor(out=dst[:, m, :], in0=dst[:, m, :], scalar=g, in1=r, op0=ALU.mult, op1=ALU.mult).then_inc(head_ready, 1)

            head_norm(B1, 0, vec("k_gain"))
            norm("ffn2", chunk(X), chunk(H), gain("ffn1_1"))
            swiglu(2)
            norm("stick", chunk(X), chunk(H), gain("mix_1"))
            head_norm(B3, 8, qg[:, 0:1])

            mask = const("stick")

            def wide(buf, c):
                return buf[:, c:c + 2, :].rearrange("p c t -> p (c t)")[:, 0:3 * P]

            for s in range(SH + 2):
                if s < SH:
                    dve.wait_ge(log1p_ready, 2 * (s + 1))
                    z, l = work[:, s % 2, 0:3 * P], work[:, 2 + s % 2, 0:3 * P]
                    sp_, stay = work[:, 4 + s % 2, 0:3 * P], wide(B6, 2 * (s % 2))
                    step(dve.scalar_tensor_tensor(out=sp_, in0=z, scalar=0.0, in1=l, op0=ALU.max, op1=ALU.add))
                    if s >= 2:
                        dve.wait_ge(stay_done, s - 1)
                    dve.scalar_tensor_tensor(out=stay, in0=sp_, scalar=-1.0, in1=mask, op0=ALU.mult, op1=ALU.mult).then_inc(stay_in, 1)
                    dve.wait_ge(stay_in, s + 1)
                    step(dve.scalar_tensor_tensor(out=sp_, in0=z, scalar=0.0, in1=l, op0=ALU.min, op1=ALU.subtract))
                if 1 <= s <= SH:
                    h = s - 1
                    dve.wait_ge(stay_done, h + 1)
                    if h >= 2:
                        dve.wait_ge(so_done, h - 1)
                    dve.tensor_tensor(wide(B5, 4 + 2 * (h % 2)), bank(6)[:, 0:3 * P], work[:, 4 + h % 2, 0:3 * P], ALU.add).then_inc(logw_ready, 1)
                if s >= 2:
                    h = s - 2
                    dve.wait_ge(w_exp, h + 1)
                    w = wide(B5, 4 + 2 * (h % 2))
                    dve.tensor_tensor(w, w, mask, ALU.mult).then_inc(w_ready, 1)
            for m in range(8):
                add_tile("bo", m)
            norm("ffn3", chunk(X), chunk(H), gain("ffn2_1"))
            swiglu(3)



def _columns(vector):
    return vector.reshape(-1, P).T


def _chunks(matrix):
    k, n = matrix.shape
    return matrix.reshape(k // P, P, n).transpose(1, 0, 2).reshape(P, -1)


def _pieces(matrix):
    return [_chunks(matrix[:, j:j + 512]) for j in range(0, matrix.shape[1], 512)]


def _vectors(i):
    def rows(a, n=P):
        out = np.zeros((P, 1), np.float32)
        out[:a.size, 0] = a
        return out

    parts = {
        "norm_mix": _columns(i["norm_mix_g"][0]), "b_glu": _columns(i["b_glu"][0]),
        "w_dw": i["w_dw"][0].reshape(TAPS * AC, P).T, "b_dw": _columns(i["b_dw"][0]),
        "ln_g": _columns(i["conv_ln_g"][0]), "ln_b": _columns(i["conv_ln_b"][0]),
        "attn_g": _columns(i["attn_out_g"][0]), "norm_mem": _columns(i["norm_mem_g"][0]),
        "mem_norm": _columns(i["mem_norm_g"][0]), "norm_ffn": _columns(i["norm_ffn_g"][0]),
        "final": _columns(i["final_g"]), "b_forget": rows(i["b_forget"][0]),
        "ffn1_0": _columns(i["ffn1_norm_2"][0]), "ffn1_1": _columns(i["ffn1_norm_2"][1]),
        "mix_0": _columns(i["mix_norm_2"][0]), "mix_1": _columns(i["mix_norm_2"][1]),
        "conv_w": i["a_conv_w_2"][0].reshape(TAPS2 * DC, P).T, "conv_b": _columns(i["a_conv_b_2"][0]),
        "b_r": _columns(i["a_b_r_2"][0]), "b_i": _columns(i["a_b_i_2"][0]),
        "lam": _columns(i["a_lambda_2"][0]), "kv": _columns(i["kv_norm_2"]),
        "k_gain": np.concatenate([i["k_norm_2"]] * 2).reshape(P, 1),
        "q_gain": np.concatenate([i["q_norm_2"][0]] * 2).reshape(P, 1),
        "ffn2_0": _columns(i["ffn2_norm_2"][0]), "ffn2_1": _columns(i["ffn2_norm_2"][1]),
        "b_route": np.broadcast_to(np.concatenate([i["b_route_group"][0], i["b_route_expert"][0].reshape(-1)]), (P, NL)),
    }
    return np.concatenate([parts[name] for name in VECTORS], 1)


def _layouts(i):
    w_in = i["w_in"][0]
    q, k, v, f, c = 0, DA, 2 * DA, 3 * DA, 3 * DA + HEADS
    stream = [_chunks(w_in[:, c + DA:c + 2 * DA]), _chunks(w_in[:, c:c + DA])]
    stream += _pieces(i["w_mkv"][0]) + [_chunks(w_in[:, a:a + DA]) for a in (q, k, v)]
    stream += _pieces(i["w_out"][0]) + _pieces(i["w_mq"][0]) + _pieces(i["w_mo"][0])
    rec = i["a_w_in_2"][0]
    stream += _pieces(rec[:, D:]) + _pieces(rec[:, :D])
    blocks = np.stack([i["a_w_r_2"][0], i["a_w_i_2"][0]]).reshape(2, NB, 2, P, 2 * P)
    stream += [blocks.transpose(3, 0, 1, 2, 4).reshape(P, SLOT)]
    stream += _pieces(i["a_w_out_2"][0]) + _pieces(i["w_kv_2"]) + _pieces(i["b_w_q_2"][0]) + _pieces(i["b_w_o_2"][0])
    ffn = []
    for l in range(2):
        for w13, w2 in ((i["ffn1_w13_2"][l], i["ffn1_w2_2"][l]), (i["ffn2_w13_2"][l], i["ffn2_w2_2"][l])):
            up = w13.reshape(DC, P, 2, FC, P).transpose(3, 1, 0, 2, 4).reshape(FC, P, 2 * D)
            ffn.append(np.concatenate([up, w2.reshape(FC, P, D)], 2))
    w_route = np.concatenate([i["w_route_group"][0], i["w_route_expert"][0].transpose(1, 0, 2).reshape(D, E)], 1)

    def experts(w):
        e, k, n = w.shape
        return w.reshape(e, k // P, P, n).transpose(0, 2, 1, 3).reshape(e, P, -1)

    return {
        "xT": _chunks(i["x"][0].T), "memT": _chunks(i["mem"][0].T), "consts": constants(), "vectors": _vectors(i),
        "w_forget": _chunks(w_in[:, f:c]), "w_route": _chunks(w_route), "stream": np.stack(stream), "ffn": np.concatenate(ffn, 0),
        "w_gate": experts(i["w_gate"][0]), "w_up": experts(i["w_up"][0]), "w_down": experts(i["w_down"][0]),
    }


def kernel(**inputs):
    import concourse.bacc as bacc
    from concourse.bass_utils import run_bass_kernel_spmd

    nc = bacc.Bacc("TRN2", target_bir_lowering=False, num_devices=1)
    arrays = {n: np.ascontiguousarray(a) for n, a in _layouts({n: np.asarray(a) for n, a in inputs.items()}).items()}
    args = {n: nc.dram_tensor(n, a.shape, F32, kind="ExternalInput").ap() for n, a in arrays.items()}
    out = nc.dram_tensor("out", (P, DC * T), F32, kind="ExternalOutput").ap()
    two_blocks(nc, *args.values(), out)
    result = run_bass_kernel_spmd(nc, [arrays], core_ids=[0]).results[0]["out"]
    return result.reshape(P, DC, T).transpose(2, 1, 0).reshape(1, T, D)
```

```python
from contextlib import ExitStack

import numpy as np

import concourse.bass as bass
from concourse import mybir

F32 = mybir.dt.float32
F32R = mybir.dt.float32r
I32 = mybir.dt.int32
ACT = mybir.ActivationFunctionType
ALU = mybir.AluOpType
AX = mybir.AxisListType

P = 128
T = 256
TT = T // P
D = 1024
DC = D // P
EPS = 1e-6
BIG = 1e30

HEADS, DH = 8, 64
DA = HEADS * DH
AC = DA // P
TAPS = 31
PAD = 32
MH, MDH = 4, 256
GROUPS, PER = 4, 8
E = GROUPS * PER
PAIRS = E // 2
FE = 512
FEC = FE // P
CAP = 64
NL = GROUPS + E
EP = E + 4
FF = 2816
FC = FF // P
NB = 4
TAPS2 = 4
SH = 16

SLOTS = 6
SLOT = 4096
FPIECE = 3 * D
UNIT = 1024
UNITS = 3

CONSTS = {}
VECTORS = {}


def columns(table, sizes):
    at = 0
    for name, n in sizes:
        table[name] = (at, n)
        at += n
    return at


NCONST = columns(CONSTS, [
    ("ident", P), ("ones", P), ("before", P), ("after", P), ("headsum", P), ("causal", 3 * P),
    ("stick", 3 * P), ("slots", CAP), ("first8", PER), ("first4", GROUPS), ("passes", 4),
    ("neghalf", TT), ("eps", 1), ("scan1", T), ("scan0", T), ("queryside", T), ("pick", 8)])
NVEC = columns(VECTORS, [
    ("norm_mix", 8), ("b_glu", 8), ("w_dw", TAPS * 4), ("b_dw", 4), ("ln_g", 4), ("ln_b", 4),
    ("attn_g", 4), ("norm_mem", 8), ("mem_norm", 8), ("norm_ffn", 8), ("final", 8), ("b_forget", 1),
    ("ffn1_0", 8), ("ffn1_1", 8), ("mix_0", 8), ("mix_1", 8), ("conv_w", TAPS2 * 8), ("conv_b", 8),
    ("b_r", 8), ("b_i", 8), ("lam", 8), ("kv", 8), ("k_gain", 1), ("q_gain", 1), ("ffn2_0", 8),
    ("ffn2_1", 8), ("b_route", NL)])


def constants():
    c = np.zeros((P, NCONST), np.float32)

    def put(name, value):
        at, n = CONSTS[name]
        c[:, at:at + n] = value

    row, col = np.arange(P)[:, None], np.arange(P)[None, :]
    put("ident", row == col)
    put("ones", 1)
    put("before", row < col)
    put("after", row > col)
    put("headsum", row // DH == col // DH)
    tri = np.where(col <= row, 0, -BIG)
    put("causal", np.concatenate([tri, np.zeros((P, P)), tri], 1))
    strict = np.where(col < row, 0, -BIG)
    put("stick", np.concatenate([strict, np.zeros((P, P)), strict], 1))
    put("slots", np.arange(CAP))
    put("first8", PER - np.arange(PER))
    put("first4", GROUPS - np.arange(GROUPS))
    put("passes", CAP * np.arange(4))
    put("neghalf", -0.5)
    put("eps", EPS)
    put("scan1", 1)
    key = np.zeros((P, 4, T), np.float32)
    pick = np.zeros((P, 2, 4), np.float32)
    for j in range(4):
        key[2 * j, j] = 1
        key[DH + 2 * j + 1, j] = 1
        pick[2 * j, 0, j] = -1
        pick[2 * j + 1, 1, j] = -1
    put("pick", pick.reshape(P, -1))
    query = np.zeros((P, T), np.float32)
    query[32:40] = 1
    query[DH + 32:DH + 40] = 1
    put("queryside", query)
    return c, key.reshape(P, -1)



class Tile:

    def __init__(self, n, bank, engine, emptied, before):
        self.n, self.bank, self.engine, self.emptied, self.before = n, bank, engine, emptied, before


class Plan:
    def __init__(self):
        self.tiles, self.stage = [], {}
        self.last = {}
        self.count = {"act": 0, "dve": 0}
        self.pieces = []
        self.first = {}
        self.filled = [0] * SLOTS
        self.units = []
        self.ufirst = {}
        self.unit_reads = 0

    def add(self, stage, engines, banks=None):
        out = []
        for i, engine in enumerate(engines):
            n = len(self.tiles)
            bank = banks[i] if banks else n % 4
            self.count[engine] += 1
            t = Tile(n, bank, engine, self.count[engine], self.last.get(bank))
            self.last[bank] = t
            self.tiles.append(t)
            out.append(t)
        self.stage[stage] = out

    def piece(self, stage, source, index, floats, freed):
        n = len(self.pieces)
        self.first.setdefault(stage, n)
        self.filled[n % SLOTS] += 16
        self.pieces.append((source, index, floats, freed, self.filled[n % SLOTS]))

    def unit(self, stage, piece, kind, index, freed):
        self.ufirst.setdefault(stage, len(self.units))
        self.units.append((piece, kind, index, freed))

    def stream(self, stage, at):
        for m, t in enumerate(self.stage[stage]):
            if m % 4 == 0:
                self.piece(stage, "stream", at + m // 4, SLOT, ("lo_ready", len(self.units) + 4))
            self.unit(stage, len(self.pieces) - 1, "columns", m % 4, ("tile_done", t.n + 1))
        return at + len(self.stage[stage]) // 4

    def stream_values(self, stage, at):
        tiles = self.stage[stage]
        for h in range(len(tiles) // TT):
            self.piece(stage, "stream", at + h, SLOT, ("lo_ready", len(self.units) + 4))
            for u in range(4):
                if u < 3:
                    self.unit_reads += 1
                    freed = ("unit_read", self.unit_reads)
                else:
                    freed = ("tile_done", tiles[TT * h + 1].n + 1)
                self.unit(stage, len(self.pieces) - 1, "rows", u, freed)
        return at + len(tiles) // TT


def make_plan():
    p = Plan()
    p.add("forget", ["dve"])
    p.add("glu", ["act", "dve"] * 4)
    p.add("q", ["act"] * 4)
    p.add("k", ["act"] * 4)
    p.add("v", ["act"] * 2)
    p.add("memk", ["act"] * 8)
    p.add("memv", ["act"] * 4)
    p.add("wout", ["dve"] * 8)
    p.add("mq", ["act"] * 8)
    p.add("mo", ["dve"] * 8)
    p.add("htok", ["act"] * 4)
    p.add("route", ["dve"])
    p.add("rank", ["dve"])
    p.add("maxrank", ["dve"])
    p.add("ffn0", ["dve"] * 4, range(4))
    p.add("rec", ["act"] * 8)
    p.add("r", ["act"] * 8)
    p.add("i", ["act"] * 8)
    p.add("gate", ["act"] * 8)
    p.add("aout", ["dve"] * 8)
    p.add("ffn1", ["dve"] * 4, range(4))
    p.add("kvk", ["act"] * 8)
    p.add("kvv", ["act"] * 4)
    p.add("ffn2", ["dve"] * 4, range(4))
    p.add("bq", ["act"] * 8)
    p.add("bo", ["dve"] * 8)
    p.add("ffn3", ["dve"] * 4, range(4))

    for j in range(2):
        p.piece("glu", "stream", j, SLOT, ("lo_ready", 7 + j))
    for m, t in enumerate(p.stage["glu"]):
        p.unit("glu", m % 2, "columns", m // 2, ("tile_done", t.n + 1))
    at = 2
    at = p.stream("q", at)
    at = p.stream("k", at)
    at = p.stream_values("v", at)
    at = p.stream("memk", at)
    at = p.stream_values("memv", at)
    at = p.stream("wout", at)
    at = p.stream("mq", at)
    at = p.stream("mo", at)
    for n in range(PAIRS):
        for source, e in [("gate", 0), ("gate", 1), ("up", 0), ("up", 1), ("down", 0), ("down", 1)]:
            freed = {"gate": ("hidden_done", 2 * n + 1), "up": ("hidden_done", 2 * n + 2), "down": ("y_done", 2 * n + 2)}[source]
            p.piece("moe", source, 2 * n + e, SLOT, freed)

    def ffn(which):
        stage, u0, n0 = f"ffn{which}", len(p.units), len(p.pieces)
        for j in range(FC):
            down = u0 + 3 * j + (4 if j < FC - 1 else 2)
            p.piece(stage, "ffn", FC * which + j, FPIECE, ("lo_ready", down + 1))
        order = [(0, 0), (1, 0)]
        for j in range(1, FC):
            order += [(0, j), (1, j), (2, j - 1)]
        order += [(2, FC - 1)]
        for part, j in order:
            if part < 2:
                freed = ("gu_done", 2 * (FC * which + j) + part + 1)
            elif j < FC - 1:
                freed = ("down_done", (FC - 1) * which + j + 1)
            else:
                freed = ("tile_done", p.stage[stage][3].n + 1)
            p.unit(stage, n0 + j, "flat", part, freed)

    ffn(0)
    at = p.stream("rec", at)
    p.piece("r", "stream", at, SLOT, ("tile_done", p.stage["i"][7].n + 1))
    at += 1
    at = p.stream("gate", at)
    at = p.stream("aout", at)
    ffn(1)
    at = p.stream("kvk", at)
    at = p.stream_values("kvv", at)
    ffn(2)
    at = p.stream("bq", at)
    at = p.stream("bo", at)
    ffn(3)
    p.streamed = at
    return p


NORMS = [("mix", 8), ("mem", 8), ("attn", 4), ("conv", 4), ("memq", 8), ("moe", 8), ("final", 8),
         ("ffn0", 8), ("lru", 8), ("ffn1", 8), ("kv", 8), ("stick", 8), ("ffn3", 8)]
NORM = {}
_at = 0
for _n, (_name, _chunks) in enumerate(NORMS):
    NORM[_name] = (_n, _chunks, _at)
    _at += _chunks

SPLITS = [("mix", 8), ("mem", 8), ("mixed", 8), ("memq", 8), ("memo", 8), ("ffn0", 8), ("lru", 8), ("aout", 8),
          ("ffn1", 8), ("kv", 8), ("ffn2", 8), ("stick", 8), ("sticko", 8), ("ffn3", 8)]
SPLIT = {name: 8 * n for n, (name, _) in enumerate(SPLITS)}


def two_blocks(nc, xT, memT, consts, keys, vectors, w_forget, w_route, stream, ffn, w_gate, w_up, w_down, out):
    plan = make_plan()
    sources = {"stream": stream, "ffn": ffn, "gate": w_gate, "up": w_up, "down": w_down}

    with ExitStack() as ctx:
        def sb(name, shape, dt=F32):
            return ctx.enter_context(nc.sbuf_tensor(name, shape, dt))

        def sem(name):
            return ctx.enter_context(nc.semaphore(name))

        ring = sb("ring", [P, SLOTS, SLOT])
        X = sb("X", [P, DC, T])
        B1 = sb("B1", [P, DC, T])
        B2 = sb("B2", [P, DC, T])
        B3 = sb("B3", [P, DC, T])
        B4 = sb("B4", [P, DC, T])
        B5 = sb("B5", [P, DC, T])
        H = B5
        Hh = sb("Hh", [P, DC, T], F32R)
        Hl = sb("Hl", [P, DC, T], F32R)
        Wh = sb("Wh", [P, UNITS, UNIT], F32R)
        Wl = sb("Wl", [P, UNITS, UNIT], F32R)
        hidh = sb("hidh", [P, 2, T], F32R)
        hidl = sb("hidl", [P, 2, T], F32R)
        zin = sb("zin", [P, DC, T + PAD])
        C = sb("C", [P, NCONST])
        V = sb("V", [P, NVEC])
        wf = sb("wf", [P, DC, HEADS])
        wr = sb("wr", [P, DC, NL])
        ms = sb("ms", [P, TT])
        rs = sb("rs", [P, TT])
        diag = sb("diag", [P, T])
        small = B5[:, 4:8, :]
        work = sb("work", [P, 4, 512])
        work2 = B4[:, 0:4, :].rearrange("p (a c) t -> p a (c t)", a=2)
        flat = work[:, :, :].rearrange("p a n -> p (a n)")

        def prob(g):
            return flat[:, (g % 3) * 3 * P:(g % 3 + 1) * 3 * P] if g < HEADS else work[:, g % 2, :]

        def turned_prob(g):
            return flat[:, (9 + 3 * (g % 2)) * P:(12 + 3 * (g % 2)) * P] if g < HEADS else work[:, 2 + g % 2, :]

        def half(buf, i, n=3 * P):
            return buf.rearrange("p c t -> p (c t)")[:, (i % 2) * 512:(i % 2) * 512 + n]

        zmask = lambda h: half(B5[:, 0:4, :], h)
        sig = lambda h: half(B4[:, 0:4, :], h)
        stay = lambda h: half(B4[:, 4:8, :], h)
        kept = lambda h: half(B5[:, 4:8, :], h, 512)
        weight = lambda h: flat[:, (h % 3) * 3 * P:(h % 3 + 1) * 3 * P]

        negmax = sb("negmax", [P, 2, TT])
        rowsum = sb("rowsum", [P, 2, TT])
        rowinv = sb("rowinv", [P, 2, TT])
        hid = B5[:, 2:4, :]
        act2 = B5[:, 0:2, :]
        spl = sb("spl", [P, 4, DC])
        qg = sb("qg", [P, 1])
        lg = sb("lg", [P, TT, NL])
        r4 = sb("r4", [P, 6, TT, GROUPS])
        r8 = sb("r8", [P, 8, TT, PER])
        r1 = sb("r1", [P, 12, TT])
        pick32 = sb("pick32", [P, TT, PER, GROUPS])
        chosen = sb("chosen", [P, TT, E])
        rank = sb("rank", [P, TT, EP])
        gates = sb("gates", [P, TT, EP])
        mr = sb("mr", [P, 2])
        mrow = sb("mrow", [1, 8])
        npass = sb("npass", [1, 1], I32)
        disp = B3[:, 4, :].rearrange("p (t e s) -> p t e s", t=TT, e=2)
        comb = B3[:, 5, :].rearrange("p (t e s) -> p t e s", t=TT, e=2)
        back = B3[:, 6, :]
        esilu = B2[:, 4:6, :].rearrange("p c t -> p (c t)")
        eprod = B2[:, 6:8, :].rearrange("p c t -> p (c t)")
        ehid = B4[:, 0:2, :].rearrange("p c (a s) -> p (c a) s", a=2)
        XG = B2[:, 0:4, :].rearrange("p c (a s) -> p (c a) s", a=2)
        Y = B3[:, 0:4, :].rearrange("p a t -> p (a t)")
        htok = B1[:, :, :].rearrange("p a t -> p (a t)").rearrange("p (t d) -> p t d", t=TT)

        ps = ctx.enter_context(nc.psum_tensor("ps", [P, 8, 512], F32))

        def bank(b):
            return ps[:, b, :]

        def const(name):
            at, n = CONSTS[name]
            return C[:, at:at + n]

        def vec(name, i=0):
            at, _ = VECTORS[name]
            return V[:, at + i:at + i + 1]

        ident, ones = const("ident"), const("ones")

        def zeros(n):
            return const("scan0")[:, 0:n]

        loaded = [sem(f"slot{i}_loaded") for i in range(SLOTS)]
        inputs_loaded = [sem(f"input{i}_loaded") for i in range(7)]
        tile_done = sem("tile_done")
        taken = {"act": sem("taken_by_act"), "dve": sem("taken_by_dve")}
        prepared = sem("prepared")
        square_done = sem("square_done")
        msum_done = sem("msum_done")
        ms_ready = sem("ms_ready")
        rs_ready = sem("rs_ready")
        diag_ready = sem("diag_ready")
        rbcast_done = sem("rbcast_done")
        normed = sem("normed")
        renormed = sem("renormed")
        hi_ready = sem("hi_ready")
        lo_ready = sem("lo_ready")
        unit_read = sem("unit_read")
        hh_ready = sem("hh_ready")
        hl_ready = sem("hl_ready")
        hidh_ready = sem("hidh_ready")
        hidl_ready = sem("hidl_ready")
        vstep = sem("vector_step")
        astep = sem("scalar_step")
        forget_exp = sem("forget_exp")
        bias_ready = sem("bias_ready")
        glu_gate = sem("glu_gate")
        conv_step = sem("conv_step")
        mean_done = sem("mean_done")
        centred = sem("centred")
        conv_out = sem("conv_out")
        score_done = sem("score_done")
        score_read = sem("score_read")
        max_ready = sem("max_ready")
        exp_done = sem("exp_done")
        prob_ready = sem("prob_ready")
        turned = sem("turned")
        turned_copied = sem("turned_copied")
        o_done = sem("o_done")
        o_copied = sem("o_copied")
        down_done = sem("down_done")
        gu_done = sem("gu_done")
        ffn_silu = sem("ffn_silu")
        hid_ready = sem("hid_ready")
        lam_ready = sem("lam_ready")
        xconv_ready = sem("xconv_ready")
        decay_ready = sem("decay_ready")
        ssq_ready = sem("ssq_ready")
        root_ready = sem("root_ready")
        lru_out = sem("lru_out")
        headsq = sem("headsq")
        headsum_done = sem("headsum_done")
        headroot = sem("headroot")
        head_ready = sem("head_ready")
        z_done = sem("z_done")
        z_ready = sem("z_ready")
        sigmoids = sem("sigmoids")
        products = sem("products")
        w_ready = sem("w_ready")
        w_turned = sem("w_turned")
        w_copied = sem("w_copied")
        so_done = sem("so_done")
        router_exp = sem("router_exp")
        router_in = sem("router_in")
        chosen_ready = sem("chosen_ready")
        maxrank_in = sem("maxrank_in")
        npass_ready = sem("npass_ready")
        stored = sem("stored")

        class Moe:

            def __init__(self, tag):
                self.disp_ready = sem(f"{tag}disp_ready")
                self.gathered = sem(f"{tag}gathered")
                self.xg_ready = sem(f"{tag}xg_ready")
                self.comb_turned = sem(f"{tag}comb_turned")
                self.back_ready = sem(f"{tag}back_ready")
                self.hidden_done = sem(f"{tag}hidden_done")
                self.esilu_ready = sem(f"{tag}esilu_ready")
                self.eprod_ready = sem(f"{tag}eprod_ready")
                self.hidden_turned = sem(f"{tag}hidden_turned")
                self.ehid_ready = sem(f"{tag}ehid_ready")
                self.y_done = sem(f"{tag}y_done")
                self.y_ready = sem(f"{tag}y_ready")
                self.spread_done = sem(f"{tag}spread_done")
                self.spread_taken = sem(f"{tag}spread_taken")

        hot, cold = Moe("main_"), Moe("more_")
        cold_loaded = sem("more_loaded")
        shifted = sem("ranks_shifted")
        by_name = {"tile_done": tile_done, "hidden_done": hot.hidden_done, "y_done": hot.y_done,
                   "down_done": down_done, "gu_done": gu_done, "lo_ready": lo_ready, "unit_read": unit_read}

        block = ctx.enter_context(nc.Block())

        def slot_of(stage, j):
            n = plan.first[stage] + j
            return n % SLOTS

        def wait_piece(eng, stage, j):
            n = plan.first[stage] + j
            eng.wait_ge(loaded[n % SLOTS], plan.pieces[n][4])

        def piece(stage, j, k):
            return ring[:, slot_of(stage, j), :].rearrange("p (k n) -> p k n", k=k)

        def wait_taken(eng, tile):
            eng.wait_ge(taken[tile.engine], tile.emptied)

        def unit_views(u):
            n, kind, index, _ = plan.units[u]
            w = ring[:, n % SLOTS, :]
            hi, lo = Wh[:, u % UNITS, :], Wl[:, u % UNITS, :]
            if kind == "columns":
                shape = lambda a: a.rearrange("p (k n) -> p k n", k=DC)
                return shape(w)[:, :, index * P:(index + 1) * P], shape(hi), shape(lo)
            return w[:, index * UNIT:(index + 1) * UNIT], hi, lo

        def moe_slots(n0=0):
            return [(plan.first["moe"] + j) % SLOTS for j in range(SLOTS)]

        S_G0, S_G1, S_U0, S_U1, S_D0, S_D1 = moe_slots()
        MOE_BASE = {(plan.first["moe"] + j) % SLOTS: plan.pieces[plan.first["moe"] + j][4] - 16 for j in range(SLOTS)}

        @block.sync
        def _(sp):
            def load(n):
                source, index, floats, _, _ = plan.pieces[n]
                if n >= SLOTS:
                    name, value = plan.pieces[n - SLOTS][3]
                    sp.wait_ge(by_name[name], value)
                sp.dma_start(ring[:, n % SLOTS, 0:floats], sources[source][index]).then_inc(loaded[n % SLOTS], 16)

            for n in range(plan.first["moe"] + SLOTS):
                load(n)

            MOE_ORDER = [(w_gate, 0), (w_gate, 1), (w_up, 0), (w_up, 1), (w_down, 0), (w_down, 1)]
            with sp.Fori(1, PAIRS) as n:
                for j, (source, e) in enumerate(MOE_ORDER):
                    s = (plan.first["moe"] + j) % SLOTS
                    if j < 4:
                        sp.wait_ge(hot.hidden_done, 2 * n - 1 + j // 2)
                    else:
                        sp.wait_ge(hot.y_done, 2 * n)
                    sp.dma_start(ring[:, s, :], source[2 * n + e]).then_inc(loaded[s], 16)
            sp.wait_ge(npass_ready, 1)
            passes = sp.value_load(npass[0:1, 0:1], min_val=1, max_val=4)
            with sp.If(passes > 1):
                sp.wait_ge(hot.y_done, E)
                with sp.Fori(1, passes) as q:
                    with sp.Fori(0, PAIRS) as n:
                        sp.wait_ge(cold.y_done, (q - 1) * E + 2 * n + 1)
                        for j, (source, e) in enumerate(MOE_ORDER):
                            s = (plan.first["moe"] + j) % SLOTS
                            sp.dma_start(ring[:, s, :], source[2 * n + e]).then_inc(cold_loaded, 16)
                sp.wait_ge(chosen_ready, 2)
            start = plan.first["ffn0"]

            def ffn_loads(which):
                base = plan.first[f"ffn{which}"]
                head = SLOTS + (FC - SLOTS) % SLOTS
                for j in range(head):
                    load(base + j)
                with sp.Fori(0, (FC - head) // SLOTS) as i:
                    for j in range(SLOTS):
                        n = base + head + j
                        sp.wait_ge(lo_ready, 3 * SLOTS * i + plan.pieces[n - SLOTS][3][1])
                        sp.dma_start(ring[:, n % SLOTS, 0:FPIECE], ffn[6 * i + FC * which + head + j]).then_inc(loaded[n % SLOTS], 16)

            n = start
            for which in range(4):
                while n < plan.first[f"ffn{which}"]:
                    load(n)
                    n += 1
                ffn_loads(which)
                n += FC
            last = plan.stage["ffn3"]
            for b in range(4):
                wait_taken(sp, last[b])
                sp.dma_start(out[:, 2 * b * T:(2 * b + 2) * T], X[:, 2 * b:2 * b + 2, :].rearrange("p c t -> p (c t)")).then_inc(stored, 16)
            sp.wait_ge(stored, 4 * 16)

        @block.gpsimd
        def _(pool):
            pool.memset(zin[:, :, 0:PAD], 0.0).then_inc(prepared, 1)
            pool.memset(rank[:, :, :], -1.0).then_inc(prepared, 1)
            pool.memset(gates[:, :, :], 0.0).then_inc(prepared, 1)
            pool.wait_ge(inputs_loaded[0], 16)
            for n in range(len(NORMS)):
                pool.wait_ge(ms_ready, n + 1)
                if n:
                    pool.wait_ge(diag_ready, TT * n)
                pool.tensor_tensor(rs[:, :], ms[:, :], const("neghalf"), ALU.pow).then_inc(rs_ready, 1)

        @block.scalar
        def _(act):
            steps = [0]
            act.nop().then_inc(hot.y_ready, 1)
            act.nop().then_inc(hot.back_ready, 1)

            def step(ins):
                ins.then_inc(astep, 1)
                steps[0] += 1
                act.wait_ge(astep, steps[0])

            for i, (dst, src) in [(2, (X[:, :, :].rearrange("p c t -> p (c t)"), xT)), (0, (C[:, :], consts)),
                                  (1, (V[:, :], vectors)), (4, (wf[:, :, :].rearrange("p c h -> p (c h)"), w_forget)),
                                  (3, (B3[:, :, :].rearrange("p c t -> p (c t)"), memT)),
                                  (5, (wr[:, :, :].rearrange("p c h -> p (c h)"), w_route))]:
                act.dma_start(dst, src).then_inc(inputs_loaded[i], 16)

            ucursor = [0]

            def split_unit(u, wait_load=True, i=None, unit_step=0, freed_step=0, load_step=0):
                plus = (lambda v, k: v) if i is None else (lambda v, k: k * i + v)
                n = plan.units[u][0]
                if wait_load:
                    act.wait_ge(loaded[n % SLOTS], plus(plan.pieces[n][4], load_step))
                if u >= UNITS:
                    name, value = plan.units[u - UNITS][3]
                    act.wait_ge(by_name[name], plus(value, freed_step))
                w, hi, _ = unit_views(u)
                act.activation(hi, w, ACT.Copy).then_inc(hi_ready, 1)

            def split_upto(limit):
                while ucursor[0] < min(limit, len(plan.units)):
                    split_unit(ucursor[0])
                    ucursor[0] += 1

            def high(name, src, ready, chunks=range(DC)):
                for c in chunks:
                    ready(c)
                    act.activation(Hh[:, c, :], src(c), ACT.Copy).then_inc(hh_ready, 1)

            def when_normed(name):
                return lambda c: act.wait_ge(normed, NORM[name][2] + c + 1)

            def chunk(buf):
                return lambda c: buf[:, c, :]

            def squares(name, src, ready, dst=H):
                n, chunks, base = NORM[name]
                if n:
                    act.wait_ge(msum_done, n)
                for c in range(chunks):
                    ready(c)
                    act.activation(dst[:, c, :], src(c), ACT.Square).then_inc(square_done, 1)

            def take(stage, i, dst, func=ACT.Copy, scale=1.0, bias=None, cols=T, rows=P):
                t = plan.stage[stage][i]
                act.wait_ge(tile_done, t.n + 1)
                extra = {} if bias is None else {"bias": bias}
                act.activation(dst, bank(t.bank)[0:rows, 0:cols], func, scale=scale, **extra).then_inc(taken["act"], 1)

            squares("mix", chunk(X), lambda c: act.wait_ge(inputs_loaded[2], 16))
            high("mix", chunk(H), when_normed("mix"))
            split_upto(UNITS)
            act.wait_ge(inputs_loaded[1], 16)
            act.wait_ge(taken["dve"], plan.stage["forget"][0].emptied)
            step(act.activation(small[0:HEADS, 1, :], small[0:HEADS, 0, :], ACT.Abs))
            step(act.activation(small[0:HEADS, 1, :], small[0:HEADS, 1, :], ACT.Exp, scale=-1.0))
            act.activation(small[0:HEADS, 2, :], small[0:HEADS, 1, :], ACT.Ln, bias=1.0).then_inc(forget_exp, 1)
            at = VECTORS["lam"][0]
            step(act.activation(spl[:, 0, :], V[:, at:at + DC], ACT.Abs))
            step(act.activation(spl[:, 0, :], spl[:, 0, :], ACT.Exp, scale=-1.0))
            act.activation(spl[:, 1, :], spl[:, 0, :], ACT.Ln, bias=1.0).then_inc(lam_ready, 1)
            u0 = plan.ufirst["glu"]
            for c in range(AC):
                t = plan.stage["glu"][2 * c]
                act.wait_ge(tile_done, t.n + 1)
                act.activation(zin[:, 4 + c, PAD:PAD + T], bank(t.bank)[:, 0:T], ACT.Sigmoid, bias=vec("b_glu", 4 + c)).then_inc(taken["act"], 1)
                split_upto(u0 + 2 * c + 2 + UNITS)
            squares("mem", chunk(B3), lambda c: act.wait_ge(inputs_loaded[3], 16), dst=B1)

            def take_all(stage, dst, **more):
                for m in range(len(plan.stage[stage])):
                    take(stage, m, dst(m), **more)
                    split_upto(plan.ufirst[stage] + m + 1 + UNITS)

            def take_values(stage, dst):
                u0 = plan.ufirst[stage]
                for m in range(len(plan.stage[stage])):
                    if m % TT == 0:
                        split_upto(u0 + 2 * m + 3 + UNITS)
                    take(stage, m, dst(m), cols=512)

            take_all("q", lambda m: B4[:, m, :], scale=DH ** -0.5)
            take_all("k", lambda m: B4[:, 4 + m, :])
            v1 = B5[:, 0:4, :].rearrange("p c t -> p (c t)").rearrange("p (t d) -> p t d", t=TT)
            take_values("v", lambda m: v1[:, m, :])
            high("mem", chunk(B3), when_normed("mem"))
            split_upto(plan.ufirst["memk"] + UNITS)
            memv = B2[:, :, :].rearrange("p c t -> p (c t)").rearrange("p (t d) -> p t d", t=TT)
            take_all("memk", lambda m: B1[:, m, :])
            act.wait_ge(hl_ready, SPLIT["mem"] + DC)
            act.dma_start(B3[:, 4:8, :].rearrange("p c t -> p (c t)"), keys).then_inc(inputs_loaded[6], 16)

            def mem_dst(m):
                return memv[:, m % 2, (m // 2) * 512:(m // 2 + 1) * 512]

            take_values("memv", mem_dst)
            split_upto(plan.ufirst["wout"] + UNITS)

            def softmax_exp(g, src, widths):
                act.wait_ge(max_ready, g + 1)
                if g >= HEADS:
                    act.wait_ge(turned, g - 1)
                at = 0
                for t, w in enumerate(widths):
                    act.activation(prob(g)[:, at:at + w], src[:, at:at + w], ACT.Exp, bias=negmax[:, g % 2, t:t + 1],
                                   accum_out=rowsum[:, g % 2, t:t + 1]).then_inc(exp_done, 1)
                    at += w

            def turned_copy(g, cols):
                act.wait_ge(turned, g + 1)
                act.activation(turned_prob(g)[:, 0:cols], bank(6)[:, 0:cols], ACT.Copy).then_inc(turned_copied, 1)

            for s in range(HEADS + 3):
                if s < HEADS:
                    softmax_exp(s, prob(s), [P, T])
                if 2 <= s < HEADS + 2:
                    turned_copy(s - 2, 3 * P)
                if s >= 4 and s % 2 == 0:
                    j = (s - 4) // 2
                    act.wait_ge(o_done, j + 1)
                    act.activation(B3[:, j, :], bank(7)[:, 0:T], ACT.Copy).then_inc(o_copied, 1)
            squares("attn", lambda c: B3[:, c, :], lambda c: act.wait_ge(o_copied, c + 1))
            high("mixed", chunk(B5), when_normed("attn"), range(AC))
            squares("conv", lambda c: B5[:, 4 + c, :], lambda c: act.wait_ge(centred, c + 1), dst=B3[:, 4:8, :])
            for c in range(AC):
                act.wait_ge(normed, NORM["conv"][2] + c + 1)
                act.activation(B5[:, 4 + c, :], B5[:, 4 + c, :], ACT.Silu, bias=vec("ln_b", c)).then_inc(conv_out, 1)
            high("mixed", chunk(B5), lambda c: act.wait_ge(conv_out, c - AC + 1), range(AC, DC))

            def residual(stage):
                return lambda c: wait_taken(act, plan.stage[stage][c])

            def squares_behind(name, stage, cap=None):
                u0 = plan.ufirst[stage]
                cap = cap or len(plan.units)

                def ready(c):
                    if c:
                        split_upto(min(cap, u0 + c + UNITS))
                    residual(stage)(c)

                squares(name, chunk(X), ready)
                split_upto(min(cap, u0 + DC + UNITS))

            squares_behind("memq", "wout")
            high("memq", chunk(H), when_normed("memq"))
            take_all("mq", lambda m: B4[:, m, :], scale=MDH ** -0.5)
            for s in range(MH + 2):
                g = HEADS + s
                if s < MH:
                    softmax_exp(g, bank(4 + g % 2), [T, T])
                if 1 <= s <= MH:
                    turned_copy(g - 1, 512)
                if s >= 2:
                    act.wait_ge(o_done, HEADS // 2 + s - 1)
                    act.activation(Hh[:, 2 * (s - 2):2 * (s - 2) + 2, :].rearrange("p c t -> p (c t)"), bank(7)[:, :], ACT.Copy).then_inc(hh_ready, 2)
            squares_behind("moe", "mo", plan.ufirst["ffn0"])
            for m in range(4):
                take("htok", m, htok[:, m // 2, (m % 2) * 512:(m % 2 + 1) * 512], cols=512)
            act.wait_ge(router_in, 1)
            act.activation(r4[:, 1, :, :], r4[:, 0, :, :], ACT.Exp).then_inc(router_exp, 1)
            act.wait_ge(router_in, 2)
            act.activation(r1[:, 6, :], r1[:, 5, :], ACT.Exp).then_inc(router_exp, 1)

            def xg_copy(S, k):
                for b in range(2):
                    act.wait_ge(S.gathered, 2 * k + b + 1)
                    act.activation(XG[:, 4 * b:4 * b + 4, :].rearrange("p c t -> p (c t)"), bank(1 + 2 * b), ACT.Copy).then_inc(S.xg_ready, 1)

            def silu(S, k):
                act.wait_ge(S.hidden_done, 2 * k + 1)
                act.activation(esilu, bank(3), ACT.Silu).then_inc(S.esilu_ready, 1)

            def hidden_copy(S, k):
                act.wait_ge(S.hidden_turned, k + 1)
                act.activation(ehid.rearrange("p f s -> p (f s)"), bank(0), ACT.Copy).then_inc(S.ehid_ready, 1)

            def back_copy(S, k):
                act.wait_ge(S.comb_turned, k + 1)
                act.activation(back[:, :], bank(2)[:, 0:T], ACT.Copy).then_inc(S.back_ready, 1)

            def y_copy(S, k, more):
                for b in range(2):
                    act.wait_ge(S.y_done, 2 * k + b + 1 + more)
                    act.activation(Y[:, b * 512:(b + 1) * 512], bank(5 + b), ACT.Copy).then_inc(S.y_ready, 1)

            xg_copy(hot, 0)
            with act.Fori(0, PAIRS) as n:
                silu(hot, n)
                hidden_copy(hot, n)
                xg_copy(hot, n + 1)
                back_copy(hot, n)
                y_copy(hot, n, 0)
            act.wait_ge(npass_ready, 1)
            passes = act.value_load(npass[0:1, 0:1], min_val=1, max_val=4)
            with act.If(passes > 1):
                with act.Fori(1, passes) as q:
                    with act.Fori(0, PAIRS) as n:
                        k = (q - 1) * PAIRS + n
                        xg_copy(cold, k)
                        back_copy(cold, k)
                        silu(cold, k)
                        hidden_copy(cold, k)
                        y_copy(cold, k, 1)
            def after_moe(c):
                act.wait_ge(chosen_ready, 2)

            squares("final", lambda c: X[:, c, :], after_moe)

            def swiglu(which):
                u0, base = plan.ufirst[f"ffn{which}"], FC * which

                def one(j, i=None):
                    plus = (lambda v, k: v) if i is None else (lambda v, k: k * i + v)

                    def split(place, kind, steps):
                        if place >= UNITS and place < 3 * FC:
                            split_unit(u0 + place, wait_load=(kind == 0), i=i, freed_step=steps, load_step=16)

                    act.wait_ge(gu_done, plus(2 * (base + j) + 1, 12))
                    act.activation(act2[:, j % 2, :], bank(4)[:, 0:T], ACT.Silu).then_inc(ffn_silu, 1)
                    if j < FC - 1:
                        split(3 * j + 2, 0, 12)
                    act.wait_ge(hid_ready, plus(base + j + 1, 6))
                    act.activation(hidh[:, j % 2, :], hid[:, j % 2, :], ACT.Copy).then_inc(hidh_ready, 1)
                    if j < FC - 1:
                        split(3 * j + 3, 1, 12)
                        split(3 * j + 4, 2, 6)
                    else:
                        split(3 * j + 2, 2, 6)

                for j in range(2):
                    one(j)
                with act.Fori(0, 3) as i:
                    for j in range(2, 8):
                        one(j, i)
                for j in range(20, FC):
                    one(j)
                ucursor[0] = u0 + 3 * FC
                split_upto(u0 + 3 * FC + 2)

            def squares_ffn(name, which):
                squares(name, chunk(X), residual_ffn(which))
                split_upto(plan.ufirst[f"ffn{which}"] + 3 * FC + UNITS)

            def residual_ffn(which):
                return lambda c: wait_taken(act, plan.stage[f"ffn{which}"][c // 2])

            squares("ffn0", chunk(X), when_normed("final"))
            split_upto(plan.ufirst["ffn0"] + UNITS)
            high("ffn0", chunk(H), when_normed("ffn0"))
            swiglu(0)

            squares_ffn("lru", 0)
            high("lru", chunk(H), when_normed("lru"))
            take_all("rec", lambda m: zin[:, m, PAD:PAD + T])
            for m in range(8):
                take("r", m, B3[:, m, :], func=ACT.Sigmoid, bias=vec("b_r", m))
            for m in range(8):
                take("i", m, B4[:, m, :], func=ACT.Sigmoid, bias=vec("b_i", m))
            act.wait_ge(lam_ready, 2)
            act.wait_ge(taken["act"], plan.stage["r"][7].emptied)
            for m in range(8):
                act.activation(B5[:, m, :], B3[:, m, :], ACT.Tanh, scale=spl[:, 3, m:m + 1]).then_inc(decay_ready, 1)
            for m in range(8):
                act.wait_ge(decay_ready, m + 1)
                act.activation(B3[:, m, :], B3[:, m, :], ACT.Exp, scale=spl[:, 3, m:m + 1]).then_inc(decay_ready, 1)
            split_upto(plan.ufirst["gate"] + 1 + UNITS)
            for m in range(8):
                act.wait_ge(ssq_ready, m + 1)
                act.activation(B5[:, m, :], B5[:, m, :], ACT.Sqrt, scale=-1.0).then_inc(root_ready, 1)
            take_all("gate", lambda m: B2[:, m, :], func=ACT.Gelu_apprx_tanh)
            high("aout", chunk(B5), lambda c: act.wait_ge(lru_out, c + 1))
            squares_behind("ffn1", "aout")
            high("ffn1", chunk(H), when_normed("ffn1"))
            swiglu(1)
            squares_ffn("kv", 1)
            high("kv", chunk(H), when_normed("kv"))

            def head_norm(stage, dst, base):
                def root(m):
                    act.wait_ge(headsum_done, base + m + 1)
                    if base + m >= 2:
                        act.wait_ge(head_ready, base + m - 1)
                    act.activation(work[:, 2 + m % 2, 0:T], bank(4 + m % 2)[:, 0:T], ACT.Sqrt, scale=1.0 / DH,
                                   bias=const("eps")).then_inc(headroot, 1)

                for m in range(8):
                    t = plan.stage[stage][m]
                    act.wait_ge(tile_done, t.n + 1)
                    act.activation(dst[:, m, :], bank(t.bank)[:, 0:T], ACT.Copy).then_inc(headsq, 1)
                    if m >= 2:
                        act.wait_ge(headsum_done, base + m - 1)
                    act.activation(work[:, m % 2, 0:T], bank(t.bank)[:, 0:T], ACT.Square).then_inc(taken["act"], 1)
                    split_upto(plan.ufirst[stage] + m + 1 + UNITS)
                    if m >= 1:
                        root(m - 1)
                root(7)

            head_norm("kvk", B1, 0)
            take_values("kvv", mem_dst)
            act.wait_ge(tile_done, plan.stage["kvv"][3].n + 1)
            high("ffn2", chunk(H), lambda c: act.wait_ge(renormed, c + 1))
            split_upto(plan.ufirst["ffn2"] + UNITS)
            swiglu(2)
            squares_ffn("stick", 2)
            high("stick", chunk(H), when_normed("stick"))
            head_norm("bq", B3, 8)

            for s in range(SH + 3):
                if s < SH:
                    act.wait_ge(z_ready, s + 1)
                    if s >= 2:
                        act.wait_ge(w_ready, 2 * (s - 1))
                    act.activation(stay(s), zmask(s), ACT.Sigmoid, scale=-1.0).then_inc(sigmoids, 1)
                    act.activation(sig(s), zmask(s), ACT.Sigmoid).then_inc(sigmoids, 1)
                if 2 <= s < SH + 2:
                    h = s - 2
                    act.wait_ge(w_turned, h + 1)
                    act.activation(turned_prob(h % 2), bank(6)[:, 0:3 * P], ACT.Copy).then_inc(w_copied, 1)
                if s >= 4 and s % 2 == 0:
                    j = (s - 4) // 2
                    act.wait_ge(so_done, j + 1)
                    act.activation(Hh[:, j, :], bank(7)[:, 0:T], ACT.Copy).then_inc(hh_ready, 1)
            squares_behind("ffn3", "bo")
            high("ffn3", chunk(H), when_normed("ffn3"))
            swiglu(3)

        @block.tensor
        def _(pe):
            def norm(name, squared):
                n, chunks, base = NORM[name]
                if n:
                    pe.wait_ge(ms_ready, n)
                for c in range(chunks):
                    pe.wait_ge(square_done, base + c + 1)
                    for t in range(TT):
                        last = pe.matmul(bank(6)[:, t:t + 1], squared[:, c, t * P:(t + 1) * P], ones[:, 0:1],
                                         start=(c == 0 and t == 0), stop=(c == chunks - 1), skip_group_check=True)
                last.then_inc(msum_done, 1)
                pe.wait_ge(diag_ready, TT * (n + 1))
                if n:
                    pe.wait_ge(normed, base)
                pe.matmul(bank(7)[:, 0:T], ones, diag[:, :], start=True, stop=True).then_inc(rbcast_done, 1)

            def open_tile(t):
                if t.before:
                    wait_taken(pe, t.before)

            def wait_unit(u):
                pe.wait_ge(lo_ready, u + 1)

            def by_high(o, u, name=None, start=True):
                _, hi, lo = unit_views(u)
                k = lambda a: a if len(a.shape) == 3 else a.rearrange("p (k n) -> p k n", k=DC)
                for c in range(DC):
                    if name:
                        pe.wait_ge(hh_ready, SPLIT[name] + c + 1)
                    pe.matmul(o, k(hi)[:, c, :], Hh[:, c, :], start=(c == 0), stop=False)
                    pe.matmul(o, k(lo)[:, c, :], Hh[:, c, :], start=False, stop=False)

            def by_low(o, u, name=None):
                _, hi, _ = unit_views(u)
                k = lambda a: a if len(a.shape) == 3 else a.rearrange("p (k n) -> p k n", k=DC)
                for c in range(DC):
                    if name:
                        pe.wait_ge(hl_ready, SPLIT[name] + c + 1)
                    last = pe.matmul(o, k(hi)[:, c, :], Hl[:, c, :], start=False, stop=(c == DC - 1))
                return last

            def project(stage, name=None, after=None):
                u0, tiles = plan.ufirst[stage], plan.stage[stage]
                for pair in [tiles[0:2]] + [[t] for t in tiles[2:]]:
                    for t in pair:
                        open_tile(t)
                        m = t.n - tiles[0].n
                        wait_unit(u0 + m)
                        by_high(bank(t.bank)[:, 0:T], u0 + m, name if m == 0 else None)
                    for t in pair:
                        m = t.n - tiles[0].n
                        by_low(bank(t.bank)[:, 0:T], u0 + m, name if m == 0 else None).then_inc(tile_done, 1)
                    if after:
                        for t in pair:
                            after(t.n - tiles[0].n)

            def values(stage):
                u0, tiles = plan.ufirst[stage], plan.stage[stage]
                for h in range(len(tiles) // TT):
                    pair = tiles[TT * h:TT * h + TT]
                    for t in pair:
                        open_tile(t)
                    for r in range(4):
                        u = u0 + 4 * h + r
                        wait_unit(u)
                        for tt, t in enumerate(pair):
                            for k in range(2):
                                c, w = 2 * r + k, slice(k * 512, (k + 1) * 512)
                                hi, lo = Wh[:, u % UNITS, w], Wl[:, u % UNITS, w]
                                tokens = slice(tt * P, (tt + 1) * P)
                                pe.matmul(bank(t.bank), Hh[:, c, tokens], hi, start=(c == 0), stop=False)
                                pe.matmul(bank(t.bank), Hh[:, c, tokens], lo, start=False, stop=False)
                                last = pe.matmul(bank(t.bank), Hl[:, c, tokens], hi, start=False, stop=(c == DC - 1))
                            if r == 3:
                                last.then_inc(tile_done, 1)
                        if r < 3:
                            last.then_inc(unit_read, 1)

            pe.nop().then_inc(cold.y_done, 1)

            pe.wait_ge(inputs_loaded[0], 16)
            norm("mix", H)
            t = plan.stage["forget"][0]
            pe.wait_ge(inputs_loaded[4], 16)
            for c in range(DC):
                pe.wait_ge(normed, NORM["mix"][2] + c + 1)
                last = pe.matmul(bank(t.bank)[0:HEADS, 0:T], wf[:, c, :], H[:, c, :], start=(c == 0), stop=(c == DC - 1))
            last.then_inc(tile_done, 1)
            project("glu", "mix")
            norm("mem", B1)
            project("q")
            project("k")
            values("v")
            project("memk", "mem")
            values("memv")

            v1 = B5[:, 0:4, :].rearrange("p c t -> p (c t)").rearrange("p (t d) -> p t d", t=TT)
            memv = B2[:, :, :].rearrange("p c t -> p (c t)").rearrange("p (t d) -> p t d", t=TT)
            keyside = B3[:, 4:8, :]
            queryside = const("queryside")

            def turn(p_, done):
                for k in range(3):
                    last = pe.transpose(bank(6)[:, k * P:(k + 1) * P], p_[:, k * P:(k + 1) * P], ident)
                last.then_inc(done, 1)

            def weigh(h, v, pt):
                r0 = (h % 2) * DH
                pe.matmul(bank(7)[r0:r0 + DH, 0:T], v[:, 0, h * DH:(h + 1) * DH], pt[:, 0:T], start=True, stop=False)
                return pe.matmul(bank(7)[r0:r0 + DH, P:T], v[:, 1, h * DH:(h + 1) * DH], pt[:, T:T + P], start=False, stop=True)

            pe.wait_ge(taken["act"], plan.stage["v"][1].emptied)
            pe.wait_ge(bias_ready, 8)
            for s in range(HEADS + 3):
                if s < HEADS:
                    c, r0 = s // 2, (s % 2) * DH
                    if s >= 2:
                        pe.wait_ge(score_read, s - 1)
                    for qt in range(TT):
                        o = bank(4 + s % 2)[:, qt * P:qt * P + P + qt * P]
                        keys = (qt + 1) * P
                        pe.matmul(o, B4[r0:r0 + DH, c, qt * P:(qt + 1) * P], B4[r0:r0 + DH, 4 + c, 0:keys], start=True, stop=False)
                        last = pe.matmul(o, queryside[r0:r0 + 40, qt * P:(qt + 1) * P], keyside[r0:r0 + 40, c, 0:keys], start=False, stop=True)
                    last.then_inc(score_done, 1)
                if 2 <= s < HEADS + 2:
                    h = s - 2
                    pe.wait_ge(prob_ready, TT * h + 2)
                    if h:
                        pe.wait_ge(turned_copied, h)
                    turn(prob(h), turned)
                if s >= 3:
                    h = s - 3
                    pe.wait_ge(turned_copied, h + 1)
                    if h % 2 == 0 and h:
                        pe.wait_ge(o_copied, h // 2)
                    last = weigh(h, v1, turned_prob(h))
                    if h % 2:
                        last.then_inc(o_done, 1)
            norm("attn", H)
            for c in range(AC):
                pe.wait_ge(conv_step, 4 * (TAPS - 1) + c + 1)
                last = pe.matmul(bank(5)[:, 0:T], ones, B5[:, 4 + c, :], start=(c == 0), stop=(c == AC - 1))
            last.then_inc(mean_done, 1)
            norm("conv", B3[:, 4:8, :])
            project("wout", "mixed")
            norm("memq", H)
            project("mq", "memq")
            pe.wait_ge(taken["act"], plan.stage["mq"][7].emptied)
            for s in range(MH + 2):
                g = HEADS + s
                if s < MH:
                    if s >= 2:
                        pe.wait_ge(exp_done, TT * (g - 1))
                    for qt in range(TT):
                        for c in range(2):
                            last = pe.matmul(bank(4 + g % 2)[:, qt * T:(qt + 1) * T], B4[:, 2 * s + c, qt * P:(qt + 1) * P],
                                             B1[:, 2 * s + c, :], start=(c == 0), stop=(c == 1))
                    last.then_inc(score_done, 1)
                if 1 <= s <= MH:
                    h = g - 1
                    pe.wait_ge(prob_ready, TT * h + 2)
                    pe.wait_ge(turned_copied, h)
                    for qt in range(TT):
                        for kt in range(TT):
                            last = pe.transpose(bank(6)[:, kt * T + qt * P:kt * T + (qt + 1) * P],
                                                work[:, h % 2, qt * T + kt * P:qt * T + (kt + 1) * P], ident)
                    last.then_inc(turned, 1)
                if s >= 2:
                    h = g - 2
                    pe.wait_ge(turned_copied, h + 1)
                    if s > 2:
                        pe.wait_ge(hl_ready, SPLIT["memo"] + 2 * (s - 2))
                    for c in range(2):
                        for kt in range(TT):
                            f0 = (2 * (s - 2) + c) * P
                            last = pe.matmul(bank(7)[:, c * T:(c + 1) * T], memv[:, kt, f0:f0 + P],
                                             work[:, 2 + h % 2, kt * T:(kt + 1) * T], start=(kt == 0), stop=(kt == 1))
                    last.then_inc(o_done, 1)
            project("mo", "memo")
            norm("moe", H)
            for m, t in enumerate(plan.stage["htok"]):
                open_tile(t)
                for c in range(4):
                    pe.wait_ge(normed, NORM["moe"][2] + (m % 2) * 4 + c + 1)
                    last = pe.transpose(bank(t.bank)[:, c * P:(c + 1) * P], H[:, (m % 2) * 4 + c, (m // 2) * P:(m // 2 + 1) * P], ident)
                last.then_inc(tile_done, 1)
            t = plan.stage["route"][0]
            open_tile(t)
            pe.wait_ge(inputs_loaded[5], 16)
            for tt in range(TT):
                for c in range(DC):
                    last = pe.matmul(bank(t.bank)[:, tt * NL:(tt + 1) * NL], H[:, c, tt * P:(tt + 1) * P], wr[:, c, :],
                                     start=(c == 0), stop=(c == DC - 1))
            last.then_inc(tile_done, 1)
            t = plan.stage["rank"][0]
            open_tile(t)
            pe.wait_ge(chosen_ready, 1)
            pe.matmul(bank(t.bank)[:, 0:E], const("before"), chosen[:, 0, :], start=True, stop=True)
            pe.matmul(bank(t.bank)[:, E:2 * E], const("before"), chosen[:, 1, :], start=True, stop=False)
            pe.matmul(bank(t.bank)[:, E:2 * E], ones, chosen[:, 0, :], start=False, stop=True).then_inc(tile_done, 1)
            t = plan.stage["maxrank"][0]
            open_tile(t)
            pe.wait_ge(maxrank_in, 1)
            pe.transpose(bank(t.bank)[0:1, 0:P], mr[:, 0:1], ident).then_inc(tile_done, 1)

            def gather(S, k):
                pe.wait_ge(S.disp_ready, 2 * k + 1)
                for b in range(2):
                    for c in range(4):
                        for tt in range(TT):
                            f0 = (4 * b + c) * P
                            last = pe.matmul(bank(1 + 2 * b)[:, c * P:(c + 1) * P], htok[:, tt, f0:f0 + P],
                                             disp[:, tt, :, :].rearrange("p e s -> p (e s)"), start=(tt == 0), stop=(tt == TT - 1))
                    last.then_inc(S.gathered, 1)

            def turn_back(S, k):
                pe.wait_ge(S.disp_ready, 2 * k + 2)
                for tt in range(TT):
                    last = pe.transpose(bank(2)[:, tt * P:(tt + 1) * P], comb[:, tt, :, :].rearrange("p e s -> p (e s)"), ident)
                last.then_inc(S.comb_turned, 1)

            def hidden(S, k, landed):
                pe.wait_ge(S.xg_ready, 2 * k + 2)
                for g, slots in enumerate([(S_G0, S_G1), (S_U0, S_U1)]):
                    for s in slots:
                        landed(s)
                    for c in range(DC):
                        for e, s in enumerate(slots):
                            w = ring[:, s, :].rearrange("p (c n) -> p c n", c=DC)
                            last = pe.matmul(bank(3 + g)[e * CAP:(e + 1) * CAP, :], XG[:, c, e * CAP:(e + 1) * CAP], w[:, c, :],
                                             start=(c == 0), stop=(c == DC - 1))
                    last.then_inc(S.hidden_done, 1)

            def turn_hidden(S, k):
                pe.wait_ge(S.eprod_ready, k + 1)
                for f in range(FEC):
                    last = pe.transpose(bank(0)[:, f * P:(f + 1) * P], eprod[:, f * P:(f + 1) * P], ident)
                last.then_inc(S.hidden_turned, 1)

            def down(S, k, landed):
                for s in (S_D0, S_D1):
                    landed(s)
                pe.wait_ge(S.ehid_ready, k + 1)
                for b in range(2):
                    for f in range(FEC):
                        for e, s in enumerate((S_D0, S_D1)):
                            w = ring[:, s, :].rearrange("p (f n) -> p f n", f=FEC)
                            last = pe.matmul(bank(5 + b)[e * CAP:(e + 1) * CAP, :], ehid[:, f, e * CAP:(e + 1) * CAP],
                                             w[:, f, b * 512:(b + 1) * 512], start=(f == 0), stop=(f == FEC - 1))
                    last.then_inc(S.y_done, 1)

            def spread(S, k, y_value, back_value):
                pe.wait_ge(S.y_ready, y_value)
                pe.wait_ge(S.back_ready, back_value)
                for r in range(4):
                    if r >= 2:
                        pe.wait_ge(S.spread_taken, 4 * k + r - 1)
                    b = 7 if r % 2 == 0 else 2
                    for j in range(2):
                        c = 2 * r + j
                        last = pe.matmul(bank(b)[:, j * T:(j + 1) * T], Y[:, c * P:(c + 1) * P], back[:, :], start=True, stop=True)
                    last.then_inc(S.spread_done, 1)

            pe.wait_ge(taken["act"], plan.stage["htok"][3].emptied)
            wait_taken(pe, plan.stage["maxrank"][0])
            gather(hot, 0)
            with pe.Fori(0, PAIRS) as n:
                def landed(s):
                    pe.wait_ge(loaded[s], 16 * n + MOE_BASE[s] + 16)

                hidden(hot, n, landed)
                spread(hot, n, 2 * n + 1, n + 1)
                turn_hidden(hot, n)
                gather(hot, n + 1)
                pe.wait_ge(hot.spread_taken, 4 * n + 4)
                turn_back(hot, n)
                down(hot, n, landed)
            spread(hot, PAIRS, 2 * PAIRS + 1, PAIRS + 1)
            pe.wait_ge(npass_ready, 1)
            passes = pe.value_load(npass[0:1, 0:1], min_val=1, max_val=4)
            with pe.If(passes > 1):
                pe.wait_ge(hot.spread_taken, 4 * (PAIRS + 1))
                pe.wait_ge(hot.xg_ready, 2 * (PAIRS + 1))
                with pe.Fori(1, passes) as q:
                    with pe.Fori(0, PAIRS) as n:
                        k = (q - 1) * PAIRS + n

                        def landed(s):
                            pe.wait_ge(cold_loaded, 96 * k + 96)

                        gather(cold, k)
                        turn_back(cold, k)
                        hidden(cold, k, landed)
                        turn_hidden(cold, k)
                        down(cold, k, landed)
                        spread(cold, k, 2 * k + 2, k + 1)
                        pe.wait_ge(cold.spread_taken, 4 * k + 4)
                        pe.nop()
            norm("final", H)

            def swiglu(which):
                u0, tiles, name = plan.ufirst[f"ffn{which}"], plan.stage[f"ffn{which}"], f"ffn{which}"

                def unit_at(part, j):
                    if part < 2:
                        return u0 + (3 * j - 1 + part if j else part)
                    return u0 + (3 * j + 4 if j < FC - 1 else 3 * j + 2)

                def wait_split(u, i):
                    pe.wait_ge(lo_ready, u + 1 if i is None else 18 * i + u + 1)

                def gate_up(j, i=None):
                    for g in range(2):
                        wait_split(unit_at(g, j), i)
                        if j:
                            value = FC * which + j
                            pe.wait_ge([ffn_silu, hid_ready][g], value if i is None else 6 * i + value)
                        by_high(bank(4 + g)[:, 0:T], unit_at(g, j), name if (g, j) == (0, 0) else None)
                        if j:
                            by_low(bank(4 + g)[:, 0:T], unit_at(g, j)).then_inc(gu_done, 1)
                    if not j:
                        for g in range(2):
                            by_low(bank(4 + g)[:, 0:T], unit_at(g, j), name if g == 0 else None).then_inc(gu_done, 1)

                def down_of(j, i=None, first=False, final=False):
                    u = unit_at(2, j)
                    wait_split(u, i)
                    hidden_value = FC * which + j + 1
                    pe.wait_ge(hidl_ready, hidden_value if i is None else 6 * i + hidden_value)
                    hi, lo = Wh[:, u % UNITS, :], Wl[:, u % UNITS, :]
                    for m in range(DC):
                        if first and m % 2 == 0:
                            open_tile(tiles[m // 2])
                        o, w = bank(m // 2)[:, (m % 2) * T:(m % 2 + 1) * T], slice(m * P, (m + 1) * P)
                        pe.matmul(o, hi[:, w], hidh[:, j % 2, :], start=(first and m % 2 == 0), stop=False, skip_group_check=True)
                        pe.matmul(o, lo[:, w], hidh[:, j % 2, :], start=False, stop=False, skip_group_check=True)
                        last = pe.matmul(o, hi[:, w], hidl[:, j % 2, :], start=False, stop=final, skip_group_check=True)
                        if final and m % 2:
                            last.then_inc(tile_done, 1)
                    if not final:
                        last.then_inc(down_done, 1)

                gate_up(0)
                gate_up(1)
                down_of(0, first=True)
                with pe.Fori(0, 3) as i:
                    for j in range(2, 8):
                        gate_up(j, i)
                        down_of(j - 1, i)
                for j in range(20, FC):
                    gate_up(j)
                    down_of(j - 1)
                down_of(FC - 1, final=True)

            norm("ffn0", H)
            swiglu(0)
            norm("lru", H)
            project("rec", "lru")
            wait_piece(pe, "r", 0)
            w = ring[:, slot_of("r", 0), :].rearrange("p (g n k m) -> p g n k m", g=2, n=NB, k=2)
            for g, stage in enumerate(["r", "i"]):
                for m, t in enumerate(plan.stage[stage]):
                    open_tile(t)
                    for k in range(2):
                        pe.wait_ge(xconv_ready, 2 * (m // 2) + k + 1)
                        last = pe.matmul(bank(t.bank)[:, 0:T], w[:, g, m // 2, k, (m % 2) * P:(m % 2 + 1) * P], B1[:, 2 * (m // 2) + k, :],
                                         start=(k == 0), stop=(k == 1))
                    last.then_inc(tile_done, 1)
            project("gate")
            project("aout", "aout")
            norm("ffn1", H)
            swiglu(1)
            norm("kv", H)

            def headsum(stage, base, m):
                pe.wait_ge(taken["act"], plan.stage[stage][m].emptied)
                if base + m >= 2:
                    pe.wait_ge(headroot, base + m - 1)
                pe.matmul(bank(4 + m % 2)[:, 0:T], const("headsum"), work[:, m % 2, 0:T], start=True, stop=True).then_inc(headsum_done, 1)

            def project_heads(stage, base, name):
                def after(m):
                    if m:
                        headsum(stage, base, m - 1)
                project(stage, name, after)
                headsum(stage, base, 7)

            project_heads("kvk", 0, "kv")
            values("kvv")
            swiglu(2)
            norm("stick", H)
            project_heads("bq", 8, "stick")

            pe.wait_ge(head_ready, 16)
            for s in range(SH + 3):
                if s < SH:
                    c, r0 = s // 2, (s % 2) * DH
                    if s >= 2:
                        pe.wait_ge(z_ready, s - 1)
                    pe.matmul(bank(4 + s % 2)[:, 0:P], B3[r0:r0 + DH, c, 0:P], B1[r0:r0 + DH, c, 0:P], start=True, stop=True)
                    pe.matmul(bank(4 + s % 2)[:, P:3 * P], B3[r0:r0 + DH, c, P:T], B1[r0:r0 + DH, c, :], start=True, stop=True).then_inc(z_done, 1)
                if 2 <= s < SH + 2:
                    h = s - 2
                    pe.wait_ge(w_ready, 2 * h + 2)
                    if h:
                        pe.wait_ge(w_copied, h)
                    turn(weight(h), w_turned)
                if s >= 3:
                    h = s - 3
                    pe.wait_ge(w_copied, h + 1)
                    if h % 2 == 0 and h:
                        pe.wait_ge(hl_ready, SPLIT["sticko"] + h // 2)
                    last = weigh(h, memv, turned_prob(h % 2))
                    if h % 2:
                        last.then_inc(so_done, 1)
            project("bo", "sticko")
            norm("ffn3", H)
            swiglu(3)

        @block.vector
        def _(dve):
            steps = [0]

            def step(ins):
                ins.then_inc(vstep, 1)
                steps[0] += 1
                dve.wait_ge(vstep, steps[0])

            ucursor = [0]

            def split_unit(u, i=None):
                dve.wait_ge(hi_ready, u + 1 if i is None else 18 * i + u + 1)
                w, hi, lo = unit_views(u)
                dve.tensor_tensor(lo, w, hi.bitcast(F32), ALU.subtract).then_inc(lo_ready, 1)

            def split_upto(limit, between=None):
                while ucursor[0] < min(limit, len(plan.units)):
                    split_unit(ucursor[0])
                    ucursor[0] += 1
                    if between:
                        between()

            lows = [0]

            def low(name, src, chunks=range(DC)):
                lows[0] = SPLIT[name] + chunks[-1] + 1
                for c in chunks:
                    dve.wait_ge(hh_ready, SPLIT[name] + c + 1)
                    dve.tensor_tensor(Hl[:, c, :], src(c), Hh[:, c, :].bitcast(F32), ALU.subtract).then_inc(hl_ready, 1)

            def norm(name, src, dst, gain, width=D):
                n, chunks, base = NORM[name]
                dve.wait_ge(msum_done, n + 1)
                if n:
                    dve.wait_ge(rs_ready, n)
                dve.tensor_scalar(ms[:, :], bank(6)[:, 0:TT], 1.0 / width, EPS, ALU.mult, ALU.add).then_inc(ms_ready, 1)
                dve.wait_ge(rs_ready, n + 1)
                if n:
                    dve.wait_ge(rbcast_done, n)
                for t in range(TT):
                    dve.tensor_scalar(diag[:, t * P:(t + 1) * P], ident, rs[:, t:t + 1], None, ALU.mult).then_inc(diag_ready, 1)
                dve.wait_ge(rbcast_done, n + 1)
                if lows[0]:
                    dve.wait_ge(hl_ready, lows[0])
                for c in range(chunks):
                    dve.scalar_tensor_tensor(out=dst(c), in0=src(c), scalar=gain(c), in1=bank(7)[:, 0:T],
                                             op0=ALU.mult, op1=ALU.mult).then_inc(normed, 1)

            def chunk(buf, first=0):
                return lambda c: buf[:, first + c, :]

            def gain(name):
                return lambda c: vec(name, c)

            def add_tile(stage, m):
                t = plan.stage[stage][m]
                dve.wait_ge(tile_done, t.n + 1)
                dve.tensor_tensor(X[:, m, :], bank(t.bank)[:, 0:T], X[:, m, :], ALU.add).then_inc(taken["dve"], 1)

            def add_all(stage, cap=None):
                cap = cap or len(plan.units)
                for m in range(8):
                    add_tile(stage, m)
                    split_upto(min(cap, plan.ufirst[stage] + m + UNITS))

            dve.wait_ge(inputs_loaded[0], 16)
            dve.wait_ge(inputs_loaded[1], 16)
            dve.wait_ge(inputs_loaded[2], 16)
            norm("mix", chunk(X), chunk(H), gain("norm_mix"))
            low("mix", chunk(H))
            split_upto(UNITS)
            t = plan.stage["forget"][0]
            dve.wait_ge(tile_done, t.n + 1)
            dve.wait_ge(hl_ready, SPLIT["mix"] + DC)
            dve.tensor_scalar(small[0:HEADS, 0, :], bank(t.bank)[0:HEADS, 0:T], vec("b_forget")[0:HEADS, :], None, ALU.add).then_inc(taken["dve"], 1)
            dve.wait_ge(forget_exp, 1)
            step(dve.scalar_tensor_tensor(out=small[0:HEADS, 3, :], in0=small[0:HEADS, 0, :], scalar=0.0, in1=small[0:HEADS, 2, :],
                                          op0=ALU.min, op1=ALU.subtract))
            queryside = const("queryside")
            step(dve.tensor_tensor_scan(queryside[0:HEADS, :], const("scan1")[0:HEADS, :], small[0:HEADS, 3, :], 0.0, ALU.mult, ALU.add))
            step(dve.tensor_copy(queryside[DH:DH + HEADS, :], queryside[0:HEADS, :]))
            at = VECTORS["lam"][0]
            dve.wait_ge(lam_ready, 1)
            step(dve.tensor_scalar(spl[:, 2, :], V[:, at:at + DC], -1.0, 0.0, ALU.mult, ALU.max))
            step(dve.tensor_tensor(spl[:, 2, :], spl[:, 2, :], spl[:, 1, :], ALU.add))
            dve.tensor_scalar(spl[:, 3, :], spl[:, 2, :], -8.0, None, ALU.mult).then_inc(lam_ready, 1)
            step(dve.tensor_scalar(qg[:, :], vec("q_gain"), DH ** -0.5, None, ALU.mult))
            dve.wait_ge(prepared, 1)
            for c in range(AC):
                split_upto(plan.ufirst["glu"] + 2 * c + 1 + UNITS)
                dve.wait_ge(taken["act"], plan.stage["glu"][2 * c].emptied)
                t = plan.stage["glu"][2 * c + 1]
                dve.wait_ge(tile_done, t.n + 1)
                dve.scalar_tensor_tensor(out=zin[:, c, PAD:PAD + T], in0=bank(t.bank)[:, 0:T], scalar=vec("b_glu", c), in1=zin[:, 4 + c, PAD:PAD + T],
                                         op0=ALU.add, op1=ALU.mult).then_inc(taken["dve"], 1)
            split_upto(plan.ufirst["glu"] + 8 + UNITS)
            dve.wait_ge(taken["dve"], plan.stage["glu"][7].emptied)
            conv = [0]

            def convolve(steps):
                for _ in range(steps):
                    k, c = conv[0] // AC, conv[0] % AC
                    if k == TAPS:
                        return
                    conv[0] += 1
                    z = zin[:, c, PAD - TAPS + 1 + k:PAD - TAPS + 1 + k + T]
                    if k == 0:
                        ins = dve.tensor_scalar(B5[:, 4 + c, :], z, vec("w_dw", 4 * k + c), vec("b_dw", c), ALU.mult, ALU.add)
                    else:
                        dve.wait_ge(conv_step, 4 * k + c - 3)
                        ins = dve.scalar_tensor_tensor(out=B5[:, 4 + c, :], in0=z, scalar=vec("w_dw", 4 * k + c), in1=B5[:, 4 + c, :],
                                                       op0=ALU.mult, op1=ALU.add)
                    ins.then_inc(conv_step, 1)

            dve.wait_ge(inputs_loaded[3], 16)
            norm("mem", chunk(B3), chunk(B3), gain("mem_norm"))
            split_upto(plan.ufirst["memk"] + UNITS - 1, lambda: convolve(5))
            low("mem", chunk(B3))
            split_upto(plan.ufirst["wout"] + UNITS, lambda: convolve(5))
            convolve(4 * TAPS)
            keyside = B3[:, 4:8, :]
            pick = const("pick").rearrange("p (a j) -> p a j", a=2)
            dve.wait_ge(inputs_loaded[6], 16)
            for a in range(2):
                for j in range(4):
                    r0 = a * DH + 32
                    last = dve.tensor_scalar(keyside[r0:r0 + HEADS, j, :], queryside[0:HEADS, :], pick[0:HEADS, a, j:j + 1], None, ALU.mult)
                    last.then_inc(bias_ready, 1)

            def softmax_scale(g, widths):
                dve.wait_ge(exp_done, TT * (g + 1))
                step(dve.reciprocal(rowinv[:, g % 2, :], rowsum[:, g % 2, :]))
                at = 0
                for t, w in enumerate(widths):
                    dve.tensor_scalar(prob(g)[:, at:at + w], prob(g)[:, at:at + w], rowinv[:, g % 2, t:t + 1], None, ALU.mult).then_inc(prob_ready, 1)
                    at += w

            for s in range(HEADS + 1):
                if s < HEADS:
                    dve.wait_ge(score_done, s + 1)
                    if s >= 3:
                        dve.wait_ge(turned, s - 2)
                    dve.tensor_tensor(prob(s), bank(4 + s % 2)[:, 0:3 * P], const("causal"), ALU.add).then_inc(score_read, 1)
                    dve.wait_ge(score_read, s + 1)
                    step(dve.tensor_reduce(negmax[:, s % 2, 0:1], prob(s)[:, 0:P], AX.X, ALU.max, negate=True))
                    dve.tensor_reduce(negmax[:, s % 2, 1:2], prob(s)[:, P:3 * P], AX.X, ALU.max, negate=True).then_inc(max_ready, 1)
                if s >= 1:
                    softmax_scale(s - 1, [P, T])
            norm("attn", chunk(B3), chunk(B5), gain("attn_g"), width=DA)
            dve.wait_ge(mean_done, 1)
            for c in range(AC):
                dve.scalar_tensor_tensor(out=B5[:, 4 + c, :], in0=bank(5)[:, 0:T], scalar=-1.0 / DA, in1=B5[:, 4 + c, :],
                                         op0=ALU.mult, op1=ALU.add).then_inc(centred, 1)
            low("mixed", chunk(B5), range(AC))
            norm("conv", chunk(B5, 4), chunk(B5, 4), gain("ln_g"), width=DA)
            low("mixed", chunk(B5), range(AC, DC))
            add_all("wout")
            norm("memq", chunk(X), chunk(H), gain("norm_mem"))
            low("memq", chunk(H))
            split_upto(plan.ufirst["mo"] + UNITS)

            def low_heads(j):
                dve.wait_ge(hh_ready, SPLIT["memo"] + 2 * j + 2)
                c = slice(2 * j, 2 * j + 2)
                dve.tensor_tensor(Hl[:, c, :].rearrange("p c t -> p (c t)"), bank(7),
                                  Hh[:, c, :].rearrange("p c t -> p (c t)").bitcast(F32), ALU.subtract).then_inc(hl_ready, 2)

            for s in range(MH + 1):
                g = HEADS + s
                if s < MH:
                    dve.wait_ge(score_done, g + 1)
                    dve.tensor_reduce(negmax[:, g % 2, :], bank(4 + g % 2).rearrange("p (t k) -> p t k", t=TT), AX.X, ALU.max,
                                      negate=True).then_inc(max_ready, 1)
                if s >= 1:
                    softmax_scale(g - 1, [T, T])
                if s >= 2:
                    low_heads(s - 2)
            low_heads(MH - 1)
            add_all("mo", plan.ufirst["ffn0"])
            norm("moe", chunk(X), chunk(H), gain("norm_ffn"))

            t = plan.stage["route"][0]
            dve.wait_ge(tile_done, t.n + 1)
            at = VECTORS["b_route"][0]
            dve.tensor_tensor(lg[:, :, :], bank(t.bank)[:, 0:TT * NL].rearrange("p (t n) -> p t n", t=TT),
                              V[:, at:at + NL].unsqueeze(1).to_broadcast([P, TT, NL]), ALU.add).then_inc(taken["dve"], 1)
            dve.wait_ge(taken["dve"], t.emptied)

            def over(ap, n):
                return ap.unsqueeze(2).to_broadcast([P, TT, n])

            def first(name, n):
                return const(name).unsqueeze(1).to_broadcast([P, TT, n])

            def top1(dist, n, name, score, best, onehot):
                step(dve.tensor_scalar(score, dist, 0.0, None, ALU.is_ge))
                step(dve.tensor_tensor(score, score, first(name, n), ALU.mult))
                step(dve.tensor_reduce(best, score, AX.X, ALU.max))
                step(dve.tensor_tensor(onehot, score, over(best, n), ALU.is_equal))

            step(dve.tensor_reduce(r1[:, 0, :], lg[:, :, 0:GROUPS], AX.X, ALU.max))
            dve.tensor_tensor(r4[:, 0, :, :], lg[:, :, 0:GROUPS], over(r1[:, 0, :], GROUPS), ALU.subtract).then_inc(router_in, 1)
            dve.wait_ge(router_in, 1)
            gsel = r4[:, 3, :, :]
            top1(r4[:, 0, :, :], GROUPS, "first4", r4[:, 2, :, :], r1[:, 1, :], gsel)
            step(dve.tensor_tensor(pick32[:, :, :, :].rearrange("p t j g -> p t g j"),
                                   lg[:, :, GROUPS:NL].rearrange("p t (g j) -> p t g j", g=GROUPS),
                                   gsel.unsqueeze(3).to_broadcast([P, TT, GROUPS, PER]), ALU.mult))
            step(dve.tensor_reduce(r8[:, 0, :, :], pick32[:, :, :, :], AX.X, ALU.add))
            step(dve.tensor_reduce(r1[:, 3, :], r8[:, 0, :, :], AX.X, ALU.max))
            step(dve.tensor_tensor(r8[:, 1, :, :], r8[:, 0, :, :], over(r1[:, 3, :], PER), ALU.subtract))
            oh1, oh2 = r8[:, 3, :, :], r8[:, 6, :, :]
            top1(r8[:, 1, :, :], PER, "first8", r8[:, 2, :, :], r1[:, 4, :], oh1)
            step(dve.scalar_tensor_tensor(out=r8[:, 4, :, :], in0=oh1, scalar=-BIG, in1=r8[:, 1, :, :], op0=ALU.mult, op1=ALU.add))
            dve.tensor_reduce(r1[:, 5, :], r8[:, 4, :, :], AX.X, ALU.max).then_inc(router_in, 1)
            dve.wait_ge(router_in, 2)
            step(dve.tensor_tensor(r8[:, 5, :, :], r8[:, 4, :, :], over(r1[:, 5, :], PER), ALU.subtract))
            top1(r8[:, 5, :, :], PER, "first8", r8[:, 2, :, :], r1[:, 4, :], oh2)
            step(dve.tensor_tensor(r8[:, 7, :, :], oh1, oh2, ALU.add))
            dve.tensor_tensor(chosen[:, :, :].rearrange("p t (g j) -> p t g j", g=GROUPS),
                              gsel.unsqueeze(3).to_broadcast([P, TT, GROUPS, PER]),
                              r8[:, 7, :, :].unsqueeze(2).to_broadcast([P, TT, GROUPS, PER]), ALU.mult).then_inc(chosen_ready, 1)
            dve.wait_ge(router_exp, 2)
            step(dve.tensor_reduce(r1[:, 2, :], r4[:, 1, :, :], AX.X, ALU.add))
            step(dve.tensor_scalar(r1[:, 7, :], r1[:, 6, :], 1.0, None, ALU.add))
            step(dve.tensor_tensor(r1[:, 7, :], r1[:, 7, :], r1[:, 2, :], ALU.mult))
            step(dve.reciprocal(r1[:, 8, :], r1[:, 7, :]))
            step(dve.tensor_tensor(r1[:, 9, :], r1[:, 8, :], r1[:, 6, :], ALU.mult))
            step(dve.tensor_tensor(r8[:, 0, :, :], oh1, over(r1[:, 8, :], PER), ALU.mult))
            step(dve.tensor_tensor(r8[:, 1, :, :], oh2, over(r1[:, 9, :], PER), ALU.mult))
            step(dve.tensor_tensor(r8[:, 0, :, :], r8[:, 0, :, :], r8[:, 1, :, :], ALU.add))
            dve.wait_ge(prepared, 3)
            step(dve.tensor_tensor(gates[:, :, 0:E].rearrange("p t (g j) -> p t g j", g=GROUPS),
                                   gsel.unsqueeze(3).to_broadcast([P, TT, GROUPS, PER]),
                                   r8[:, 0, :, :].unsqueeze(2).to_broadcast([P, TT, GROUPS, PER]), ALU.mult))
            t = plan.stage["rank"][0]
            dve.wait_ge(tile_done, t.n + 1)
            dve.wait_ge(chosen_ready, 1)
            dve.scalar_tensor_tensor(out=rank[:, :, 0:E], in0=bank(t.bank)[:, 0:TT * E].rearrange("p (t e) -> p t e", t=TT), scalar=1.0,
                                     in1=chosen[:, :, :], op0=ALU.add, op1=ALU.mult).then_inc(taken["dve"], 1)
            dve.wait_ge(taken["dve"], t.emptied)
            step(dve.tensor_scalar(rank[:, :, 0:E], rank[:, :, 0:E], -1.0, None, ALU.add))
            dve.tensor_reduce(mr[:, 0:1], rank[:, :, :].rearrange("p t e -> p (t e)"), AX.X, ALU.max).then_inc(maxrank_in, 1)
            t = plan.stage["maxrank"][0]
            dve.wait_ge(tile_done, t.n + 1)
            dve.tensor_reduce(mrow[0:1, 0:1], bank(t.bank)[0:1, 0:P], AX.X, ALU.max).then_inc(taken["dve"], 1)
            dve.wait_ge(taken["dve"], t.emptied)
            step(dve.tensor_scalar(mrow[0:1, 4:8], const("passes")[0:1, :], mrow[0:1, 0:1], None, ALU.is_le))
            step(dve.tensor_reduce(mrow[0:1, 1:2], mrow[0:1, 4:8], AX.X, ALU.add))
            dve.tensor_copy(npass[:, :], mrow[0:1, 1:2]).then_inc(npass_ready, 1)

            slots = const("slots").unsqueeze(1).unsqueeze(1).to_broadcast([P, TT, 2, CAP])

            def dispatch(S, k, n):
                dve.tensor_tensor(disp[:, :, :, :], slots, rank[:, :, bass.ds(2 * n, 2)].unsqueeze(3).to_broadcast([P, TT, 2, CAP]),
                                  ALU.is_equal).then_inc(S.disp_ready, 1)

            def combine(S, k, n):
                dve.wait_ge(S.disp_ready, 2 * k + 1)
                dve.tensor_tensor(comb[:, :, :, :], disp[:, :, :, :],
                                  gates[:, :, bass.ds(2 * n, 2)].unsqueeze(3).to_broadcast([P, TT, 2, CAP]), ALU.mult).then_inc(S.disp_ready, 1)

            def expert_hidden(S, k):
                dve.wait_ge(S.esilu_ready, k + 1)
                dve.wait_ge(S.hidden_done, 2 * k + 2)
                dve.tensor_tensor(eprod, esilu, bank(4), ALU.mult).then_inc(S.eprod_ready, 1)

            def collect(S, k):
                for r in range(4):
                    dve.wait_ge(S.spread_done, 4 * k + r + 1)
                    xs = X[:, 2 * r:2 * r + 2, :].rearrange("p c t -> p (c t)")
                    dve.tensor_tensor(xs, bank(7 if r % 2 == 0 else 2), xs, ALU.add).then_inc(S.spread_taken, 1)

            dve.memset(Y, 0.0).then_inc(vstep, 1)
            dve.memset(back, 0.0).then_inc(vstep, 1)
            steps[0] += 2
            dispatch(hot, 0, 0)
            combine(hot, 0, 0)
            dve.wait_ge(hot.gathered, 2)
            dve.wait_ge(hot.disp_ready, 2)
            dispatch(hot, 1, 1)
            with dve.Fori(0, PAIRS) as n:
                expert_hidden(hot, n)
                collect(hot, n)
                dve.wait_ge(hot.comb_turned, n + 1)
                combine(hot, n + 1, n + 1)
                dve.wait_ge(hot.gathered, 2 * n + 4)
                dve.wait_ge(hot.disp_ready, 2 * n + 4)
                dispatch(hot, n + 2, n + 2)
            collect(hot, PAIRS)
            dve.wait_ge(hot.spread_taken, 4 * PAIRS + 4)
            dve.wait_ge(npass_ready, 1)
            passes = dve.value_load(npass[0:1, 0:1], min_val=1, max_val=4)
            with dve.If(passes > 1):
                dve.wait_ge(hot.disp_ready, 2 * PAIRS + 3)
                with dve.Fori(1, passes) as q:
                    dve.tensor_scalar(rank[:, :, :], rank[:, :, :], -float(CAP), None, ALU.add).then_inc(shifted, 1)
                    with dve.Fori(0, PAIRS) as n:
                        k = (q - 1) * PAIRS + n
                        dve.wait_ge(shifted, q)
                        dispatch(cold, k, n)
                        combine(cold, k, n)
                        expert_hidden(cold, k)
                        collect(cold, k)
                        dve.wait_ge(cold.gathered, 2 * k + 2)
                        dve.wait_ge(cold.comb_turned, k + 1)
                        dve.wait_ge(cold.disp_ready, 2 * k + 2)
                        dve.wait_ge(cold.spread_taken, 4 * k + 4)
            dve.nop().then_inc(chosen_ready, 1)
            norm("final", chunk(X), chunk(X), gain("final"))

            def swiglu(which):
                u0, base = plan.ufirst[f"ffn{which}"], FC * which

                def one(j, i=None):
                    plus = (lambda v, k: v) if i is None else (lambda v, k: k * i + v)

                    def split(place):
                        if place >= UNITS:
                            split_unit(u0 + place, i)

                    if j < FC - 1:
                        split(3 * j + 2)
                    dve.wait_ge(ffn_silu, plus(base + j + 1, 6))
                    dve.wait_ge(gu_done, plus(2 * (base + j) + 2, 12))
                    dve.tensor_tensor(hid[:, j % 2, :], act2[:, j % 2, :], bank(5)[:, 0:T], ALU.mult).then_inc(hid_ready, 1)
                    dve.wait_ge(hidh_ready, plus(base + j + 1, 6))
                    dve.tensor_tensor(hidl[:, j % 2, :], hid[:, j % 2, :], hidh[:, j % 2, :].bitcast(F32), ALU.subtract).then_inc(hidl_ready, 1)
                    if j < FC - 1:
                        split(3 * j + 3)
                        split(3 * j + 4)
                    else:
                        split(3 * j + 2)

                for j in range(2):
                    one(j)
                with dve.Fori(0, 3) as i:
                    for j in range(2, 8):
                        one(j, i)
                for j in range(20, FC):
                    one(j)
                ucursor[0] = u0 + 3 * FC
                split_upto(u0 + 3 * FC + 2)
                for b, t in enumerate(plan.stage[f"ffn{which}"]):
                    dve.wait_ge(tile_done, t.n + 1)
                    xs = X[:, 2 * b:2 * b + 2, :].rearrange("p c t -> p (c t)")
                    dve.scalar_tensor_tensor(out=xs, in0=bank(b), scalar=0.5, in1=xs, op0=ALU.mult, op1=ALU.add).then_inc(taken["dve"], 1)

            norm("ffn0", chunk(X), chunk(H), gain("ffn1_0"))
            split_upto(plan.ufirst["ffn0"] + UNITS)
            low("ffn0", chunk(H))
            swiglu(0)
            norm("lru", chunk(X), chunk(H), gain("mix_0"))
            low("lru", chunk(H))
            split_upto(plan.ufirst["rec"] + UNITS)
            for m in range(8):
                wait_taken(dve, plan.stage["rec"][m])
                for k in range(TAPS2):
                    z = zin[:, m, PAD - TAPS2 + 1 + k:PAD - TAPS2 + 1 + k + T]
                    if k == 0:
                        step(dve.tensor_scalar(B1[:, m, :], z, vec("conv_w", 8 * k + m), vec("conv_b", m), ALU.mult, ALU.add))
                    else:
                        ins = dve.scalar_tensor_tensor(out=B1[:, m, :], in0=z, scalar=vec("conv_w", 8 * k + m), in1=B1[:, m, :],
                                                       op0=ALU.mult, op1=ALU.add)
                        if k < TAPS2 - 1:
                            step(ins)
                        else:
                            ins.then_inc(xconv_ready, 1)
                split_upto(plan.ufirst["rec"] + m + 1 + UNITS)
            for m in range(8):
                wait_taken(dve, plan.stage["i"][m])
                dve.wait_ge(xconv_ready, m + 1)
                step(dve.tensor_tensor(B4[:, m, :], B4[:, m, :], B1[:, m, :], ALU.mult))
            for m in range(8):
                dve.wait_ge(decay_ready, DC + m + 1)
                if m >= 2:
                    dve.wait_ge(ssq_ready, m - 1)
                square = work[:, m % 2, 0:T]
                step(dve.tensor_tensor(square, B3[:, m, :], B3[:, m, :], ALU.mult))
                dve.scalar_tensor_tensor(out=B5[:, m, :], in0=square, scalar=1.0, in1=B5[:, m, :],
                                         op0=ALU.add, op1=ALU.mult).then_inc(ssq_ready, 1)
            u0 = plan.ufirst["gate"]
            split_upto(u0 + 1 + UNITS)
            for m in range(8):
                dve.wait_ge(root_ready, m + 1)
                step(dve.tensor_tensor(B4[:, m, :], B4[:, m, :], B5[:, m, :], ALU.mult))
                step(dve.tensor_tensor_scan(B5[:, m, :], B3[:, m, :], B4[:, m, :], 0.0, ALU.mult, ALU.add))
                split_upto(u0 + m + 1 + UNITS)
                wait_taken(dve, plan.stage["gate"][m])
                dve.tensor_tensor(B5[:, m, :], B5[:, m, :], B2[:, m, :], ALU.mult).then_inc(lru_out, 1)
            low("aout", chunk(B5))
            add_all("aout")
            norm("ffn1", chunk(X), chunk(H), gain("ffn2_0"))
            low("ffn1", chunk(H))
            split_upto(plan.ufirst["ffn1"] + UNITS)
            swiglu(1)
            norm("kv", chunk(X), chunk(H), gain("kv"))
            low("kv", chunk(H))
            split_upto(plan.ufirst["kvk"] + UNITS)
            dve.wait_ge(hl_ready, SPLIT["kv"] + DC)
            for c in range(DC):
                dve.scalar_tensor_tensor(out=H[:, c, :], in0=X[:, c, :], scalar=vec("ffn1_1", c), in1=bank(7)[:, 0:T],
                                         op0=ALU.mult, op1=ALU.mult).then_inc(renormed, 1)

            def head_norm(stage, dst, base, g):
                for m in range(8):
                    split_upto(plan.ufirst[stage] + m + 1 + UNITS)
                    dve.wait_ge(headroot, base + m + 1)
                    dve.wait_ge(headsq, base + m + 1)
                    r = work2[:, m % 2, 0:T]
                    step(dve.reciprocal(r, work[:, 2 + m % 2, 0:T]))
                    dve.scalar_tensor_tensor(out=dst[:, m, :], in0=dst[:, m, :], scalar=g, in1=r, op0=ALU.mult, op1=ALU.mult).then_inc(head_ready, 1)

            head_norm("kvk", B1, 0, vec("k_gain"))
            split_upto(plan.ufirst["ffn2"] + UNITS - 1)
            low("ffn2", chunk(H))
            split_upto(plan.ufirst["ffn2"] + UNITS)
            swiglu(2)
            norm("stick", chunk(X), chunk(H), gain("mix_1"))
            low("stick", chunk(H))
            split_upto(plan.ufirst["bq"] + UNITS)
            head_norm("bq", B3, 8, qg[:, 0:1])

            def low_pair(j):
                dve.wait_ge(hh_ready, SPLIT["sticko"] + j + 1)
                dve.tensor_tensor(Hl[:, j, :], bank(7)[:, 0:T], Hh[:, j, :].bitcast(F32), ALU.subtract).then_inc(hl_ready, 1)

            for i in range(2):
                for key_end in (P, P + 32 + T):
                    dve.memset(kept(i)[:, key_end:key_end + 1], 1.0).then_inc(vstep, 1)
            steps[0] += 4
            dve.wait_ge(vstep, steps[0])
            for s in range(SH + 3):
                if s < SH:
                    dve.wait_ge(z_done, s + 1)
                    if s >= 2:
                        dve.wait_ge(sigmoids, 2 * (s - 1))
                    dve.tensor_tensor(zmask(s), bank(4 + s % 2)[:, 0:3 * P], const("stick"), ALU.add).then_inc(z_ready, 1)
                if 1 <= s <= SH:
                    h = s - 1
                    dve.wait_ge(sigmoids, 2 * h + 2)
                    if h >= 2:
                        dve.wait_ge(w_ready, 2 * h - 2)
                    for at, k0, n in ((0, 0, P), (P, P + 32, T)):
                        dve.tensor_tensor_scan(kept(h)[:, k0:k0 + n][:, ::-1], stay(h)[:, at:at + n][:, ::-1], zeros(n), 1.0,
                                               ALU.mult, ALU.add).then_inc(products, 1)
                    dve.wait_ge(products, 2 * h + 2)
                    if h >= 3:
                        dve.wait_ge(w_turned, h - 2)
                    for at, k0, n in ((0, 0, P), (P, P + 32, T)):
                        dve.tensor_tensor(weight(h)[:, at:at + n], kept(h)[:, k0 + 1:k0 + 1 + n], sig(h)[:, at:at + n], ALU.mult).then_inc(w_ready, 1)
                if s >= 4 and s % 2 == 0:
                    low_pair((s - 4) // 2)
            add_all("bo")
            norm("ffn3", chunk(X), chunk(H), gain("ffn2_1"))
            low("ffn3", chunk(H))
            split_upto(plan.ufirst["ffn3"] + UNITS)
            swiglu(3)



def _columns(vector):
    return vector.reshape(-1, P).T


def _chunks(matrix):
    k, n = matrix.shape
    return matrix.reshape(k // P, P, n).transpose(1, 0, 2).reshape(P, -1)


def _pieces(matrix):
    return [_chunks(matrix[:, j:j + 512]) for j in range(0, matrix.shape[1], 512)]


def _vectors(i):
    def rows(a, n=P):
        out = np.zeros((P, 1), np.float32)
        out[:a.size, 0] = a
        return out

    parts = {
        "norm_mix": _columns(i["norm_mix_g"][0]), "b_glu": _columns(i["b_glu"][0]),
        "w_dw": i["w_dw"][0].reshape(TAPS * AC, P).T, "b_dw": _columns(i["b_dw"][0]),
        "ln_g": _columns(i["conv_ln_g"][0]), "ln_b": _columns(i["conv_ln_b"][0]),
        "attn_g": _columns(i["attn_out_g"][0]), "norm_mem": _columns(i["norm_mem_g"][0]),
        "mem_norm": _columns(i["mem_norm_g"][0]), "norm_ffn": _columns(i["norm_ffn_g"][0]),
        "final": _columns(i["final_g"]), "b_forget": rows(i["b_forget"][0]),
        "ffn1_0": _columns(i["ffn1_norm_2"][0]), "ffn1_1": _columns(i["ffn1_norm_2"][1]),
        "mix_0": _columns(i["mix_norm_2"][0]), "mix_1": _columns(i["mix_norm_2"][1]),
        "conv_w": i["a_conv_w_2"][0].reshape(TAPS2 * DC, P).T, "conv_b": _columns(i["a_conv_b_2"][0]),
        "b_r": _columns(i["a_b_r_2"][0]), "b_i": _columns(i["a_b_i_2"][0]),
        "lam": _columns(i["a_lambda_2"][0]), "kv": _columns(i["kv_norm_2"]),
        "k_gain": np.concatenate([i["k_norm_2"]] * 2).reshape(P, 1),
        "q_gain": np.concatenate([i["q_norm_2"][0]] * 2).reshape(P, 1),
        "ffn2_0": _columns(i["ffn2_norm_2"][0]), "ffn2_1": _columns(i["ffn2_norm_2"][1]),
        "b_route": np.broadcast_to(np.concatenate([i["b_route_group"][0], i["b_route_expert"][0].reshape(-1)]), (P, NL)),
    }
    return np.concatenate([parts[name] for name in VECTORS], 1)


def _layouts(i):
    w_in = i["w_in"][0]
    q, k, v, f, c = 0, DA, 2 * DA, 3 * DA, 3 * DA + HEADS
    stream = [_chunks(w_in[:, c + DA:c + 2 * DA]), _chunks(w_in[:, c:c + DA])]
    stream += [_chunks(w_in[:, a:a + DA]) for a in (q, k, v)] + _pieces(i["w_mkv"][0])
    stream += _pieces(i["w_out"][0]) + _pieces(i["w_mq"][0]) + _pieces(i["w_mo"][0])
    rec = i["a_w_in_2"][0]
    stream += _pieces(rec[:, D:])
    blocks = np.stack([i["a_w_r_2"][0], i["a_w_i_2"][0]]).reshape(2, NB, 2, P, 2 * P)
    stream += [blocks.transpose(3, 0, 1, 2, 4).reshape(P, SLOT)]
    stream += _pieces(rec[:, :D])
    stream += _pieces(i["a_w_out_2"][0]) + _pieces(i["w_kv_2"]) + _pieces(i["b_w_q_2"][0]) + _pieces(i["b_w_o_2"][0])
    ffn = []
    for l in range(2):
        for w13, w2 in ((i["ffn1_w13_2"][l], i["ffn1_w2_2"][l]), (i["ffn2_w13_2"][l], i["ffn2_w2_2"][l])):
            up = w13.reshape(DC, P, 2, FC, P).transpose(3, 1, 2, 0, 4).reshape(FC, P, 2 * D)
            ffn.append(np.concatenate([up, w2.reshape(FC, P, D)], 2))
    w_route = np.concatenate([i["w_route_group"][0], i["w_route_expert"][0].transpose(1, 0, 2).reshape(D, E)], 1)

    def experts(w):
        e, k, n = w.shape
        return w.reshape(e, k // P, P, n).transpose(0, 2, 1, 3).reshape(e, P, -1)

    return {
        "xT": _chunks(i["x"][0].T), "memT": _chunks(i["mem"][0].T), "consts": constants()[0], "keys": constants()[1], "vectors": _vectors(i),
        "w_forget": _chunks(w_in[:, f:c]), "w_route": _chunks(w_route), "stream": np.stack(stream), "ffn": np.concatenate(ffn, 0),
        "w_gate": experts(i["w_gate"][0]), "w_up": experts(i["w_up"][0]), "w_down": experts(i["w_down"][0]),
    }


def kernel(**inputs):
    import concourse.bacc as bacc
    from concourse.bass_utils import run_bass_kernel_spmd

    nc = bacc.Bacc("TRN2", target_bir_lowering=False, num_devices=1, dynamic_dma_scratch_size=1024)
    arrays = {n: np.ascontiguousarray(a) for n, a in _layouts({n: np.asarray(a) for n, a in inputs.items()}).items()}
    args = {n: nc.dram_tensor(n, a.shape, F32, kind="ExternalInput").ap() for n, a in arrays.items()}
    out = nc.dram_tensor("out", (P, DC * T), F32, kind="ExternalOutput").ap()
    two_blocks(nc, *args.values(), out)
    result = run_bass_kernel_spmd(nc, [arrays], core_ids=[0]).results[0]["out"]
    return result.reshape(P, DC, T).transpose(2, 1, 0).reshape(1, T, D)
```
